# Optimizing a Trainium2 kernel written in Bass

```python
import jax, jax.numpy as jnp
from jax import lax
import numpy as np
import math

D_MODEL = 1024
BATCH = 1
SEQ = 256
DEPTH = 2

D_FF = 2816
RET_HEADS = 4
RET_QK_DIM = 128
RET_V_DIM = 128
RET_CHUNK = 128
MLA_HEADS = 8
MLA_NOPE = 64
MLA_ROPE = 32
MLA_V = 64
Q_LORA = 256
KV_LORA = 128
Q_BLOCK = 128
ROPE_THETA = 10000.0
EPS = 1e-6
RET_Q_W = RET_HEADS * RET_QK_DIM
RET_V_W = RET_HEADS * RET_V_DIM
IN_SPLITS = [RET_Q_W, RET_Q_W, RET_V_W, RET_V_W, Q_LORA, KV_LORA, MLA_ROPE]
IN_WIDTH = sum(IN_SPLITS)
IN_OFFSETS = list(np.cumsum(IN_SPLITS)[:-1])
MIX_WIDTH = RET_HEADS * RET_V_DIM + MLA_HEADS * MLA_V


def rms_norm(x, g):
    xf = x.astype(jnp.float32)
    y = xf * lax.rsqrt(jnp.mean(xf * xf, axis=-1, keepdims=True) + EPS)
    return (y * g.astype(jnp.float32)).astype(x.dtype)

def rope_tables(positions, dim):
    inv = 1.0 / (ROPE_THETA ** (jnp.arange(0, dim, 2, dtype=jnp.float32) / dim))
    ang = positions.astype(jnp.float32)[..., None] * inv
    return jnp.cos(ang)[:, :, None, :], jnp.sin(ang)[:, :, None, :]

def apply_rope(x, cos, sin):
    xf = x.astype(jnp.float32)
    x1, x2 = jnp.split(xf, 2, axis=-1)
    return jnp.concatenate([x1 * cos - x2 * sin, x2 * cos + x1 * sin], axis=-1).astype(x.dtype)

def swiglu_ffn(h, w_gate, w_up, w_down):
    return (jax.nn.silu(h @ w_gate) * (h @ w_up)) @ w_down

def retention(q, k, v, g, gn, cos, sin):
    out_dtype = v.dtype
    B, S, H, dk = q.shape
    n = S // RET_CHUNK
    C = RET_CHUNK
    q = apply_rope(q, cos, sin).astype(jnp.float32)
    k = apply_rope(k, cos, sin).astype(jnp.float32) * (dk ** -0.5)
    v = v.astype(jnp.float32)

    def chunk(t):
        return t.reshape(B, n, C, H, -1).transpose(0, 3, 1, 2, 4)

    qc, kc, vc = chunk(q), chunk(k), chunk(v)
    lg = jnp.log(1.0 - 2.0 ** (-5.0 - jnp.arange(H, dtype=jnp.float32)))
    idx = jnp.arange(C, dtype=jnp.float32)
    rel = idx[:, None] - idx[None, :]
    decay = jnp.where(rel >= 0, jnp.exp(jnp.maximum(rel, 0.0)[None] * lg[:, None, None]), 0.0)
    scores = jnp.einsum('bhncd,bhnmd->bhncm', qc, kc) * decay[None, :, None]
    y_intra = jnp.einsum('bhncm,bhnme->bhnce', scores, vc)
    zeta = jnp.exp((C - 1 - idx)[None, :] * lg[:, None])
    chunk_kv = jnp.einsum('bhncd,bhnce->bhnde', kc * zeta[None, :, None, :, None], vc)
    chunk_decay = jnp.exp(C * lg)[None, :, None, None]

    def step(state, kv_n):
        return state * chunk_decay + kv_n, state

    init = jnp.zeros((B, H, dk, vc.shape[-1]), jnp.float32)
    _, prev = lax.scan(step, init, jnp.moveaxis(chunk_kv, 2, 0))
    prev = jnp.moveaxis(prev, 0, 2)
    xi = jnp.exp((idx + 1.0)[None, :] * lg[:, None])
    y_cross = jnp.einsum('bhncd,bhnde->bhnce', qc, prev) * xi[None, :, None, :, None]
    y = (y_intra + y_cross).transpose(0, 2, 3, 1, 4).reshape(B, S, H, -1)
    y = rms_norm(y, gn) * jax.nn.silu(g.astype(jnp.float32))
    return y.reshape(B, S, -1).astype(out_dtype)

def mla_attention(c_q, c_kv, k_rope, q_lat_norm, w_uq, kv_lat_norm, w_ukv,
                  qn_nope, qn_rope, kn_nope, kn_rope, cos, sin):
    B, S, _ = c_q.shape
    q = (rms_norm(c_q, q_lat_norm) @ w_uq).reshape(B, S, MLA_HEADS, MLA_NOPE + MLA_ROPE)
    kv = (rms_norm(c_kv, kv_lat_norm) @ w_ukv).reshape(B, S, MLA_HEADS, MLA_NOPE + MLA_V)
    q_nope, q_rope = q[..., :MLA_NOPE], q[..., MLA_NOPE:]
    k_nope, v = kv[..., :MLA_NOPE], kv[..., MLA_NOPE:]
    q_nope = rms_norm(q_nope, qn_nope)
    q_rope = apply_rope(rms_norm(q_rope, qn_rope), cos, sin)
    k_nope = rms_norm(k_nope, kn_nope)
    k_rope = apply_rope(rms_norm(k_rope[:, :, None, :], kn_rope), cos, sin)
    k_rope = jnp.broadcast_to(k_rope, (B, S, MLA_HEADS, MLA_ROPE))
    qf = jnp.concatenate([q_nope, q_rope], -1).transpose(0, 2, 1, 3).astype(jnp.float32)
    kf = jnp.concatenate([k_nope, k_rope], -1).transpose(0, 2, 1, 3).astype(jnp.float32)
    vf = v.transpose(0, 2, 1, 3).astype(jnp.float32)
    scale = (MLA_NOPE + MLA_ROPE) ** -0.5
    n_blk = S // Q_BLOCK
    q_blocks = qf.reshape(B, MLA_HEADS, n_blk, Q_BLOCK, -1).transpose(2, 0, 1, 3, 4)
    key_pos = jnp.arange(S)

    def block(args):
        qb, bi = args
        s = jnp.einsum('bhqd,bhkd->bhqk', qb, kf) * scale
        qpos = bi * Q_BLOCK + jnp.arange(Q_BLOCK)
        s = jnp.where(qpos[:, None] >= key_pos[None, :], s, -1e30)
        p = jax.nn.softmax(s, axis=-1)
        return jnp.einsum('bhqk,bhkd->bhqd', p, vf)

    o = lax.map(block, (q_blocks, jnp.arange(n_blk)))
    o = o.transpose(1, 0, 3, 2, 4).reshape(B, S, MLA_HEADS * MLA_V)
    return o.astype(c_q.dtype)

def first_inputs(seed: int = 0) -> dict:
    key = jax.random.key(seed)
    ks = iter(jax.random.split(key, 32))
    L, D, F = DEPTH, D_MODEL, D_FF

    def w(shape, fan_in):
        return jax.random.normal(next(ks), shape, jnp.float32) * (fan_in ** -0.5)

    def gain(shape):
        return 1.0 + 0.02 * jax.random.normal(next(ks), shape, jnp.float32)

    x = jax.random.normal(next(ks), (BATCH, SEQ, D), jnp.float32)
    positions = jnp.broadcast_to(jnp.arange(SEQ, dtype=jnp.int32)[None], (BATCH, SEQ))
    return {
        "x": x,
        "positions": positions,
        "ffn1_norm": gain((L, D)),
        "ffn1_w_gate": w((L, D, F), D),
        "ffn1_w_up": w((L, D, F), D),
        "ffn1_w_down": w((L, F, D), F),
        "mix_norm": gain((L, D)),
        "w_in": w((L, D, IN_WIDTH), D),
        "ret_head_norm": gain((L, RET_HEADS, RET_V_DIM)),
        "q_lat_norm": gain((L, Q_LORA)),
        "w_uq": w((L, Q_LORA, MLA_HEADS * (MLA_NOPE + MLA_ROPE)), Q_LORA),
        "kv_lat_norm": gain((L, KV_LORA)),
        "w_ukv": w((L, KV_LORA, MLA_HEADS * (MLA_NOPE + MLA_V)), KV_LORA),
        "qn_nope": gain((L, MLA_NOPE)),
        "qn_rope": gain((L, MLA_ROPE)),
        "kn_nope": gain((L, MLA_NOPE)),
        "kn_rope": gain((L, MLA_ROPE)),
        "w_o": w((L, MIX_WIDTH, D), MIX_WIDTH),
        "ffn2_norm": gain((L, D)),
        "ffn2_w_gate": w((L, D, F), D),
        "ffn2_w_up": w((L, D, F), D),
        "ffn2_w_down": w((L, F, D), F),
    }

def first_block(x, positions, ffn1_norm, ffn1_w_gate, ffn1_w_up, ffn1_w_down, mix_norm,
              w_in, ret_head_norm, q_lat_norm, w_uq, kv_lat_norm, w_ukv,
              qn_nope, qn_rope, kn_nope, kn_rope, w_o,
              ffn2_norm, ffn2_w_gate, ffn2_w_up, ffn2_w_down):
    B, S, _ = x.shape
    cos_r, sin_r = rope_tables(positions, RET_QK_DIM)
    cos_m, sin_m = rope_tables(positions, MLA_ROPE)
    for l in range(DEPTH):
        x = x + 0.5 * swiglu_ffn(rms_norm(x, ffn1_norm[l]), ffn1_w_gate[l], ffn1_w_up[l], ffn1_w_down[l])
        h = rms_norm(x, mix_norm[l])
        proj = h @ w_in[l]
        rq, rk, rv, rg, c_q, c_kv, k_rope = jnp.split(proj, IN_OFFSETS, axis=-1)
        y_ret = retention(rq.reshape(B, S, RET_HEADS, RET_QK_DIM), rk.reshape(B, S, RET_HEADS, RET_QK_DIM),
                          rv.reshape(B, S, RET_HEADS, RET_V_DIM), rg.reshape(B, S, RET_HEADS, RET_V_DIM),
                          ret_head_norm[l], cos_r, sin_r)
        y_mla = mla_attention(c_q, c_kv, k_rope, q_lat_norm[l], w_uq[l], kv_lat_norm[l], w_ukv[l],
                              qn_nope[l], qn_rope[l], kn_nope[l], kn_rope[l], cos_m, sin_m)
        x = x + jnp.concatenate([y_ret, y_mla], axis=-1) @ w_o[l]
        x = x + 0.5 * swiglu_ffn(rms_norm(x, ffn2_norm[l]), ffn2_w_gate[l], ffn2_w_up[l], ffn2_w_down[l])
    return x


DEPTH_2 = 1

GRID_W = 64
ATTN_HEADS = 8
ATTN_KV_HEADS = 2
GQA_GROUP = ATTN_HEADS // ATTN_KV_HEADS
HEAD_DIM = 64
ROPE_AXIS_DIM = HEAD_DIM // 2
HGRN_HEADS = 4
HGRN_DK = 128
HGRN_DV = 128
HGRN_CHUNK = 32
HGRN_SCALE = HGRN_DK ** -0.5
N_GROUPS = 4
EXPERTS_PER_GROUP = 8
N_EXPERTS = N_GROUPS * EXPERTS_PER_GROUP
TOP_K = 2
D_EXPERT = 512

ATTN_Q_W = ATTN_HEADS * HEAD_DIM
ATTN_KV_W = ATTN_KV_HEADS * HEAD_DIM
HGRN_K_W = HGRN_HEADS * HGRN_DK
HGRN_V_W = HGRN_HEADS * HGRN_DV
IN_SPLITS_2 = (ATTN_Q_W, ATTN_KV_W, ATTN_KV_W, HGRN_K_W, HGRN_K_W, HGRN_K_W, HGRN_V_W, HGRN_V_W, D_MODEL, D_MODEL)
D_IN = sum(IN_SPLITS_2)
SPLIT_POINTS = tuple(int(s) for s in np.cumsum(IN_SPLITS_2)[:-1])


def rmsnorm(x, g):
    xf = x.astype(jnp.float32)
    y = xf * lax.rsqrt(jnp.mean(xf * xf, axis=-1, keepdims=True) + EPS)
    return (y * g.astype(jnp.float32)).astype(x.dtype)

def axial_rope_tables(seq):
    rows = seq // GRID_W
    row_ids = jnp.repeat(jnp.arange(rows), GRID_W).astype(jnp.float32)
    col_ids = jnp.tile(jnp.arange(GRID_W), rows).astype(jnp.float32)
    inv_freq = ROPE_THETA ** (-jnp.arange(0, ROPE_AXIS_DIM, 2, dtype=jnp.float32) / ROPE_AXIS_DIM)
    ang = jnp.concatenate([row_ids[:, None] * inv_freq, col_ids[:, None] * inv_freq], axis=-1)
    return jnp.cos(ang), jnp.sin(ang)

def apply_rope_2(x, cos, sin):
    xr = x.astype(jnp.float32).reshape(x.shape[:-1] + (HEAD_DIM // 2, 2))
    a, b = xr[..., 0], xr[..., 1]
    out = jnp.stack([a * cos - b * sin, a * sin + b * cos], axis=-1)
    return out.reshape(x.shape).astype(x.dtype)

def bidir_gqa(q, k, v, q_norm, k_norm):
    B, S, _ = q.shape
    q = rmsnorm(q.reshape(B, S, ATTN_KV_HEADS, GQA_GROUP, HEAD_DIM), q_norm)
    k = rmsnorm(k.reshape(B, S, ATTN_KV_HEADS, HEAD_DIM), k_norm)
    v = v.reshape(B, S, ATTN_KV_HEADS, HEAD_DIM)
    cos, sin = axial_rope_tables(S)
    q = apply_rope_2(q, cos[:, None, None, :], sin[:, None, None, :])
    k = apply_rope_2(k, cos[:, None, :], sin[:, None, :])
    nb = S // Q_BLOCK
    qb = q.reshape(B, nb, Q_BLOCK, ATTN_KV_HEADS, GQA_GROUP, HEAD_DIM).transpose(1, 0, 3, 4, 2, 5)
    kt = k.transpose(0, 2, 1, 3)
    vt = v.transpose(0, 2, 1, 3)
    scale = HEAD_DIM ** -0.5

    def one_block(qblk):
        s = jnp.einsum('bhgqd,bhkd->bhgqk', qblk, kt).astype(jnp.float32) * scale
        p = jax.nn.softmax(s, axis=-1).astype(vt.dtype)
        return jnp.einsum('bhgqk,bhkd->bhgqd', p, vt)

    o = lax.map(one_block, qb)
    return o.transpose(1, 0, 4, 2, 3, 5).reshape(B, S, ATTN_Q_W)

def gla_chunkwise(q, k, v, log_f):
    B, H, S, dk = q.shape
    dv = v.shape[-1]
    nc = S // HGRN_CHUNK
    C = HGRN_CHUNK
    q = q.reshape(B, H, nc, C, dk)
    k = k.reshape(B, H, nc, C, dk)
    v = v.reshape(B, H, nc, C, dv)
    b = jnp.cumsum(log_f.reshape(B, H, nc, C, dk), axis=3)
    b_last = b[:, :, :, C - 1:, :]
    b_ref = b[:, :, :, C // 2:C // 2 + 1, :]
    a = jnp.einsum('bhnck,bhnsk->bhncs', q * jnp.exp(b - b_ref), k * jnp.exp(b_ref - b))
    mask = jnp.tril(jnp.ones((C, C), dtype=bool))
    o_intra = jnp.einsum('bhncs,bhnsv->bhncv', jnp.where(mask, a, 0.0), v)
    q_inter = q * jnp.exp(b)
    k_state = k * jnp.exp(b_last - b)
    decay = jnp.exp(b_last[:, :, :, 0, :])
    xs = (jnp.moveaxis(q_inter, 2, 0), jnp.moveaxis(k_state, 2, 0), jnp.moveaxis(v, 2, 0), jnp.moveaxis(decay, 2, 0))

    def step(state, inp):
        qi, ks, vv, d = inp
        o = jnp.einsum('bhck,bhkv->bhcv', qi, state)
        state = d[..., None] * state + jnp.einsum('bhck,bhcv->bhkv', ks, vv)
        return state, o

    s0 = jnp.zeros((B, H, dk, dv), jnp.float32)
    _, o_inter = lax.scan(step, s0, xs)
    o = o_intra + jnp.moveaxis(o_inter, 0, 2)
    return o.reshape(B, H, S, dv)

def hgrn2_bidir(hq, f_fwd, f_bwd, i_in, out_gate, lb_f, lb_b, hgrn_norm):
    B, S, _ = hq.shape

    def heads(t, d):
        return t.reshape(B, S, HGRN_HEADS, d).transpose(0, 2, 1, 3).astype(jnp.float32)

    q = heads(jax.nn.silu(hq.astype(jnp.float32)) * HGRN_SCALE, HGRN_DK)
    v = heads(i_in, HGRN_DV)

    def direction(f_logits, lb, flip):
        z = f_logits.astype(jnp.float32)
        f = lb + (1.0 - lb) * jax.nn.sigmoid(z)
        k = heads((1.0 - lb) * jax.nn.sigmoid(-z), HGRN_DK)
        log_f = heads(jnp.log(f), HGRN_DK)
        if flip:
            o = gla_chunkwise(jnp.flip(q, 2), jnp.flip(k, 2), jnp.flip(v, 2), jnp.flip(log_f, 2))
            return jnp.flip(o, 2)
        return gla_chunkwise(q, k, v, log_f)

    o = direction(f_fwd, lb_f, False) + direction(f_bwd, lb_b, True)
    o = rmsnorm(o.transpose(0, 2, 1, 3), hgrn_norm)
    o = o * jax.nn.silu(out_gate.reshape(B, S, HGRN_HEADS, HGRN_DV).astype(jnp.float32))
    return o.reshape(B, S, HGRN_V_W).astype(hq.dtype)

def hier_moe(h, w_rg, b_rg, w_re, b_re, w_gate, w_up, w_down):
    B, S, D = h.shape
    t = h.reshape(B * S, D)
    g_prob = jax.nn.softmax((t @ w_rg + b_rg).astype(jnp.float32), axis=-1)
    p_g, g_idx = lax.top_k(g_prob, 1)
    e_logits = (t @ w_re + b_re).astype(jnp.float32).reshape(-1, N_GROUPS, EXPERTS_PER_GROUP)
    e_sel = jnp.take_along_axis(e_logits, g_idx[:, :, None], axis=1)[:, 0]
    p_e, e_idx = lax.top_k(jax.nn.softmax(e_sel, axis=-1), TOP_K)
    p_e = p_e / jnp.sum(p_e, axis=-1, keepdims=True)
    expert_ids = g_idx * EXPERTS_PER_GROUP + e_idx
    combine = p_g * p_e
    dense_w = jnp.sum(jax.nn.one_hot(expert_ids, N_EXPERTS, dtype=jnp.float32) * combine[..., None], axis=1)
    dense_w = dense_w.astype(t.dtype)
    y = jnp.zeros((B * S, D), jnp.float32)
    for e in range(N_EXPERTS):
        hid = jax.nn.silu(t @ w_gate[e]) * (t @ w_up[e])
        y = y + ((hid * dense_w[:, e:e + 1]) @ w_down[e]).astype(jnp.float32)
    return y.reshape(B, S, D).astype(h.dtype)

def second_inputs(seed: int = 0) -> dict:
    key = jax.random.key(seed)
    ks = jax.random.split(key, 20)
    f32 = jnp.float32
    L = DEPTH_2

    def nrm(k, shape, scale):
        return jax.random.normal(k, shape, f32) * scale

    return {
        "x": nrm(ks[0], (BATCH, SEQ, D_MODEL), 1.0),
        "g_mix": 1.0 + nrm(ks[1], (L, D_MODEL), 0.02),
        "w_in": nrm(ks[2], (L, D_MODEL, D_IN), D_MODEL ** -0.5),
        "q_norm": 1.0 + nrm(ks[3], (L, HEAD_DIM), 0.02),
        "k_norm": 1.0 + nrm(ks[4], (L, HEAD_DIM), 0.02),
        "hgrn_norm": 1.0 + nrm(ks[5], (L, HGRN_DV), 0.02),
        "lb_fwd": nrm(ks[6], (L + 1, HGRN_K_W), 0.5),
        "lb_bwd": nrm(ks[7], (L + 1, HGRN_K_W), 0.5),
        "w_attn_branch": nrm(ks[8], (L, ATTN_Q_W, D_MODEL), ATTN_Q_W ** -0.5),
        "w_hgrn_branch": nrm(ks[9], (L, HGRN_V_W, D_MODEL), HGRN_V_W ** -0.5),
        "w_out": nrm(ks[10], (L, D_MODEL, D_MODEL), D_MODEL ** -0.5),
        "g_ffn": 1.0 + nrm(ks[11], (L, D_MODEL), 0.02),
        "w_router_group": nrm(ks[12], (L, D_MODEL, N_GROUPS), D_MODEL ** -0.5),
        "b_router_group": nrm(ks[13], (L, N_GROUPS), 0.01),
        "w_router_expert": nrm(ks[14], (L, D_MODEL, N_EXPERTS), D_MODEL ** -0.5),
        "b_router_expert": nrm(ks[15], (L, N_EXPERTS), 0.01),
        "w_exp_gate": nrm(ks[16], (L, N_EXPERTS, D_MODEL, D_EXPERT), D_MODEL ** -0.5),
        "w_exp_up": nrm(ks[17], (L, N_EXPERTS, D_MODEL, D_EXPERT), D_MODEL ** -0.5),
        "w_exp_down": nrm(ks[18], (L, N_EXPERTS, D_EXPERT, D_MODEL), D_EXPERT ** -0.5),
    }

def second_block(x, g_mix, w_in, q_norm, k_norm, hgrn_norm, lb_fwd, lb_bwd, w_attn_branch, w_hgrn_branch,
              w_out, g_ffn, w_router_group, b_router_group, w_router_expert, b_router_expert,
              w_exp_gate, w_exp_up, w_exp_down):
    lbs_f = jnp.cumsum(jax.nn.softmax(lb_fwd.astype(jnp.float32), axis=0), axis=0)
    lbs_b = jnp.cumsum(jax.nn.softmax(lb_bwd.astype(jnp.float32), axis=0), axis=0)
    for l in range(DEPTH_2):
        h = rmsnorm(x, g_mix[l])
        proj = h @ w_in[l]
        aq, ak, av, hq, hf_f, hf_b, hi, hg, gate_a, gate_b = jnp.split(proj, SPLIT_POINTS, axis=-1)
        attn_o = bidir_gqa(aq, ak, av, q_norm[l], k_norm[l])
        hgrn_o = hgrn2_bidir(hq, hf_f, hf_b, hi, hg, lbs_f[l], lbs_b[l], hgrn_norm[l])
        merged = (jax.nn.sigmoid(gate_a) * (attn_o @ w_attn_branch[l])
                  + jax.nn.sigmoid(gate_b) * (hgrn_o @ w_hgrn_branch[l]))
        x = x + merged @ w_out[l]
        h = rmsnorm(x, g_ffn[l])
        x = x + hier_moe(h, w_router_group[l], b_router_group[l], w_router_expert[l], b_router_expert[l],
                         w_exp_gate[l], w_exp_up[l], w_exp_down[l])
    return x


def setup_inputs(seed=0):
    out = dict(first_inputs(seed))
    for name, value in second_inputs(seed + 1).items():
        if name != "x":
            out[name + "_2"] = value
    return out


def reference(
    x, positions, ffn1_norm, ffn1_w_gate, ffn1_w_up, ffn1_w_down, mix_norm, w_in, ret_head_norm,
    q_lat_norm, w_uq, kv_lat_norm, w_ukv, qn_nope, qn_rope, kn_nope, kn_rope, w_o, ffn2_norm,
    ffn2_w_gate, ffn2_w_up, ffn2_w_down, g_mix_2, w_in_2, q_norm_2, k_norm_2, hgrn_norm_2,
    lb_fwd_2, lb_bwd_2, w_attn_branch_2, w_hgrn_branch_2, w_out_2, g_ffn_2, w_router_group_2,
    b_router_group_2, w_router_expert_2, b_router_expert_2, w_exp_gate_2, w_exp_up_2,
    w_exp_down_2,
):
    x = first_block(
        x, positions, ffn1_norm, ffn1_w_gate, ffn1_w_up, ffn1_w_down, mix_norm, w_in,
        ret_head_norm, q_lat_norm, w_uq, kv_lat_norm, w_ukv, qn_nope, qn_rope, kn_nope, kn_rope,
        w_o, ffn2_norm, ffn2_w_gate, ffn2_w_up, ffn2_w_down,
    )
    return second_block(
        x, g_mix_2, w_in_2, q_norm_2, k_norm_2, hgrn_norm_2, lb_fwd_2, lb_bwd_2,
        w_attn_branch_2, w_hgrn_branch_2, w_out_2, g_ffn_2, w_router_group_2, b_router_group_2,
        w_router_expert_2, b_router_expert_2, w_exp_gate_2, w_exp_up_2, w_exp_down_2,
    )


_drawn_inputs = setup_inputs


def setup_inputs(seed=0):
    import zlib

    import numpy as np

    out = dict(_drawn_inputs(seed))
    spreads = {}
    factors = {'ret_head_norm': 3.318,
     'q_lat_norm': 7.483,
     'kv_lat_norm': 6.282,
     'qn_nope': 5.081,
     'qn_rope': 8.0,
     'kn_nope': 8.0,
     'kn_rope': 8.0,
     'g_mix_2': 3.902,
     'q_norm_2': 8.0,
     'k_norm_2': 8.0,
     'hgrn_norm_2': 18.97,
     'lb_fwd_2': 3.49,
     'lb_bwd_2': 3.903,
     'b_router_group_2': 30.456,
     'b_router_expert_2': 64.0,
     'g_ffn_2': 8.0,
     'w_router_group_2': 3.465,
     'w_router_expert_2': 3.402,
     'w_exp_gate_2': 3.228,
     'w_exp_up_2': 3.019,
     'w_exp_down_2': 3.013}
    for name, (base, spread) in spreads.items():
        noise = np.random.default_rng([zlib.crc32(name.encode()), seed]).standard_normal(out[name].shape)
        drawn = base * np.exp(spread * noise) if base else spread * noise
        out[name] = __import__('jax').numpy.asarray(drawn.astype(out[name].dtype))
    for name, factor in factors.items():
        out[name] = (out[name] * factor).astype(out[name].dtype)
    return out
```

```python
import math
from contextlib import ExitStack

import numpy as np

import concourse.bass as bass
from concourse import mybir

ACT = mybir.ActivationFunctionType
ALU = mybir.AluOpType
F32 = mybir.dt.float32
F32R = mybir.dt.float32r
I32 = mybir.dt.int32
AX = mybir.AxisListType.X

P = 128
D = 1024
S = 256
T = S // P
KC = D // P
F = 2816
EPS = 1e-6
DEPTH = 2
BATCH_FFN = F // (2 * P)
BATCH_MID = 6
HALF = 1024
SLOTS = 6
LN10000 = math.log(10000.0)


CB = 416
RH, RD = 4, 128
MH, NOPE, ROPE = 8, 64, 32
QD = NOPE + ROPE
LAT = 384
NF = RD // 2 + ROPE // 2
MLA_SCALE = QD ** -0.5


AH, AKV, AD = 8, 2, 64
GH, GD, GC = 4, 128, 32
NCH = S // GC
CPT = P // GC
BATCH_MIX2 = 10

NG, EG, NE, FE = 4, 8, 32, 512
BS = 32
Q = P // BS
MAXB = 2 * S // BS + NE
FK = FE // P
LOGITS = NG + NE
RING = 3


def constants():
    lg = np.log(1.0 - 2.0 ** (-5.0 - np.arange(RH, dtype=np.float64)))
    m, c = np.arange(P)[:, None, None], np.arange(S)[None, None, :]
    rel = (c - m).astype(np.float64)
    decay = np.where(rel >= 0, np.exp(np.maximum(rel, 0) * lg[None, :, None]), 0.0) * RD ** -0.5
    keep = np.where(np.arange(P)[:, None] >= np.arange(P)[None, :], 0.0, -1e30)
    mask = np.concatenate([keep, np.zeros((P, P)), keep], axis=1)
    inv = [1.0 / (np.float32(10000.0) ** (np.arange(0, d, 2, dtype=np.float32) / np.float32(d))) for d in (RD, ROPE)]
    freq = np.broadcast_to(np.concatenate(inv).astype(np.float32), (P, NF))
    ids = [np.repeat(np.arange(S // 64), 64), np.tile(np.arange(64), S // 64)]
    fr = np.float32(10000.0) ** (-np.arange(0, AD // 2, 2, dtype=np.float32) / np.float32(AD // 2))
    angle = np.concatenate([i.astype(np.float32)[:, None] * fr for i in ids], axis=1)
    axial = np.stack([np.cos(angle), np.sin(angle)]).reshape(2, T, P, AD // 2).transpose(2, 0, 1, 3)
    same = np.arange(P)[:, None] // GC == np.arange(P)[None, :] // GC
    later = np.arange(P)[None, :] >= np.arange(P)[:, None]
    reach = np.stack([same & later, same & later.T], axis=1).astype(np.int32)
    carry = np.broadcast_to((np.arange(HALF) % GC != 0).astype(np.float32), (P, HALF))
    p, k = np.arange(P)[:, None], np.arange(MAXB + 1)[None, :]
    slots = p % BS + BS * k
    ids = np.arange(NE)[None, :]
    parts = [ids - 64, BS * k, slots, BS * np.arange(1, S // BS)[None, :], ids]
    route = np.concatenate([np.broadcast_to(w, (P, w.shape[1])) for w in parts], axis=1).astype(np.float32)
    before = np.triu(np.ones((P, P)), 1)
    stack = p % BS == np.arange(BS)[None, :]
    square = np.concatenate([before, np.ones((P, P)), stack], axis=1).astype(np.float32)
    return {"route": np.ascontiguousarray(route), "square": square, "axial": np.ascontiguousarray(axial.astype(np.float32)), "reach": reach, "carry": np.ascontiguousarray(carry),
            "ident": np.eye(P, dtype=np.float32), "decay": decay.astype(np.float32),
            "causal": mask.astype(np.float32), "freq": np.ascontiguousarray(freq)}


TWO_PI = (6.28125, 1.9350051879882812e-3, 3.019916050561733e-7)
PI_BELOW = 3.1415925


def program(nc, a, out, stages):
    with ExitStack() as ctx:
        def sb(name, shape, dt=F32):
            return ctx.enter_context(nc.sbuf_tensor(name, shape, dt))

        def sem(name):
            return ctx.enter_context(nc.semaphore(name))

        base = (nc.sbuf_base + 31) // 32 * 32
        KB = 1024

        def at(name, shape, kb, dt=F32):
            return nc.alloc_sbuf_tensor_at(name, shape, dt, offset=base + int(kb * KB))

        raw = at("raw", [P, 2, 3, 2 * HALF], 0)
        whi = at("whi", [P, SLOTS, HALF], 48, F32R)
        wlo = at("wlo", [P, SLOTS, HALF], 72, F32R)
        x = at("x", [P, T, D], 96)
        xn = at("xn", [P, T, D], 104)
        hhi = at("hhi", [P, KC, S], 112, F32R)
        hlo = at("hlo", [P, KC, S], 120, F32R)
        gain = at("gain", [P, D], 128)
        th = at("th", [P, 2, S], 132)
        sg = at("sg", [P, 2, S], 134)
        act_f = at("act_f", [P, 2, S], 136)
        act_hi = at("act_hi", [P, 2, S], 138, F32R)
        act_lo = at("act_lo", [P, 2, S], 140, F32R)
        y = at("y", [P, T, D], 142)
        qkT = at("qkT", [P, 2, RH, S], 150)
        rows = at("rows", [P, 2, T, RH * RD], 158)
        v = at("v", [P, T, RH * RD], 166)
        gg = at("gg", [P, T, RH * RD], 170)
        scT = at("scT", [P, RH, 3 * P], 174)
        lat_hi = at("lat_hi", [P, 3, S], 180, F32R)
        lat_lo = at("lat_lo", [P, 3, S], 183, F32R)
        q = at("q", [P, T, MH * QD], 186)
        kvs = at("kvs", [P, T, MH * P], 132)
        b4 = at("b4", [P, T, CB], 104)
        latn = at("latn", [P, T, LAT], 107.5)
        krn = at("krn", [P, T, ROPE], 110.5)
        krt = at("krt", [P, T, ROPE], 110.75)
        tmp = at("tmp", [P, T, RH * RD], 142)
        sq = at("sq", [P, T, 2 * LAT], 158)
        sqq = at("sqq", [P, T, MH * QD], 104)
        sqk = at("sqk", [P, T, MH * NOPE], 120)
        kf = at("kf", [P, T, MH * QD], 174)
        qrt = at("qrt", [P, T, MH * ROPE], 124)
        qfT = at("qfT", [P, MH, S], 112)
        kfT = at("kfT", [P, MH, S], 120)
        prob = at("prob", [P, MH, 3 * P], 150)
        probT = at("probT", [P, MH * 3, P], 162)
        g_q2 = at("g_q2", [P, GH, S], 132)
        g_e = at("g_e", [P, GH, S], 136)
        g_ee = [g_e, at("g_e1", [P, GH, S], 180)]
        g_kh1 = at("g_kh1", [P, GH, S], 136)
        g_kk = at("g_kk", [P, GH, S], 140)
        g_b = at("g_b", [P, GH, S], 144)
        g_t = at("g_t", [P, GH, S], 148)
        g_qh = at("g_qh", [P, GH, S], 152)
        g_kh = at("g_kh", [P, GH, S], 156)
        g_ks = at("g_ks", [P, GH, S], 160)
        g_qi = [at(f"g_qi{d}", [P, GH, S], 164 + 4 * d) for d in range(2)]
        g_v = at("g_v", [P, T, GH * GD], 172)
        g_ksr = [at(f"g_ksr{d}", [P, T, GH * GD], 176 + 4 * d) for d in range(2)]
        g_aT = [at(f"g_aT{d}", [P, T, GH * P], 184 + 4 * d) for d in range(2)]
        NST = 3
        state = at("state", [P, NST, GH * GD], 104)
        reach = at("reach", [P, 2, P], 110, I32)
        g_64 = at("g_64", [P, 2, AD], 128)
        aqkv = at("aqkv", [P, T, 768], 192.5)
        axial = at("axial", [P, 2, T, AD // 2], 198.5)
        g_hn = at("g_hn", [P, GD], 199)
        g_g = at("g_g", [P, T, GH * GD], 199.5)
        lb_in = at("lb_in", [P, 2, 2, GH], 205.375)
        lb = at("lb", [P, 2, 2, GH], 205.4375)
        dec = at("dec", [P, 2, GH, NCH], 205.5)
        carry = at("carry", [P, HALF], 128)
        a_w = at("a_w", [P, T, 640], 144)
        aT_q = at("aT_q", [P, AH, S], 148)
        aT_k = at("aT_k", [P, AKV, S], 156)
        a_pr = at("a_pr", [P, 4, T, S], 158)
        a_pT = at("a_pT", [P, 16, P], 166)
        a_sq = at("a_sq", [P, T, 640], 144)
        yy = at("yy", [P, T, D], 104)
        gate = [at(f"gate{c}", [P, T, 512], 132 + 4 * c) for c in range(4)]
        merged = at("merged", [P, T, D], 176)
        h_sq = at("h_sq", [P, T, 512], 184)
        ident = at("ident", [P, P], 192)
        decay = at("decay", [P, RH, S], 192.5)
        causal = at("causal", [P, 3 * P], 196.5)
        cos_r = at("cos_r", [P, T, RD // 2], 198)
        sin_r = at("sin_r", [P, T, RD // 2], 198.5)
        cos_m = at("cos_m", [P, T, ROPE // 2], 199)
        sin_m = at("sin_m", [P, T, ROPE // 2], 199.125)
        g_ret = at("g_ret", [P, RH * RD], 199.25)
        g_lat = at("g_lat", [P, LAT], 201.25)
        g_q = at("g_q", [P, QD], 202.75)
        g_k = at("g_k", [P, QD], 203.125)
        small = at("small", [P, 6, 64], 203.5)
        expert_w = [[at(f"expert_w{e}{w}", [P, 4 * HALF], kb + 16 * w) for w in range(3)] for e, kb in enumerate((0, 48, 142))]
        hcol = at("hcol", [P, KC, S], 112)
        logits = at("logits", [P, T, LOGITS], 120)
        pick = at("pick", [P, T, 2, NE], 121)
        both = at("both", [P, T, NE], 122)
        place = at("place", [P, T, 2, NE], 122.25)
        e8 = at("e8", [P, T, NE], 122.75)
        g4 = at("g4", [P, T, 6, NG], 123)
        x8 = at("x8", [P, T, 6, EG], 123.25)
        blocks = at("blocks", [P, 3, NE], 123.75)
        over = at("over", [P, NE, S // BS - 1], 125)
        cum = at("cum", [P, NE + 1], 124.25, I32)
        one = at("one", [P, T, 12], 124.5)
        diag = at("diag", [P, 8, P], 126)
        gu_sb = at("gu_sb", [P, 2, FE], 132)
        y_sb = at("y_sb", [P, D], 136)
        h_e = at("h_e", [P, KC, BS], 140)
        e_th = at("e_th", [P, FK, BS], 141)
        e_sg = at("e_sg", [P, FK, BS], 141.5)
        e_hid = at("e_hid", [P, FK, BS], 190)
        take = at("take", [P, T, BS], 190.5)
        take2 = at("take2", [P, T, BS], 190.75)
        w_router = at("w_router", [P, KC, NE], 200)
        w_group = at("w_group", [P, KC, NG], 201)
        b_router = at("b_router", [P, LOGITS], 201.25)
        route = at("route", [P, 2 * NE + 2 * (MAXB + 1) + S // BS - 1], 192.5)
        square = at("square", [P, 2 * P + BS], 193.5)
        rows4 = at("rows4", [P, 4, S], 194.75)
        give = at("give", [P, S], 198.75)
        give2 = at("give2", [P, S], 191)
        rel = at("rel", [P, T, 2, MAXB + 1], 202.25)
        pos_i = at("pos_i", [P, T], 205, I32)
        ang = at("ang", [P, T, NF], 142)
        turns = at("turns", [P, T, NF], 143)
        freq = at("freq", [P, NF], 144)
        sums = at("sums", [P, 2, MH, T], 205.25)
        bank = [ctx.enter_context(nc.psum_tensor(f"bank{i}", [P, 512], F32)) for i in range(8)]
        Y = bank[0:4]
        GU = bank[4:6]
        TR = [bank[6], bank[7], bank[4], bank[5]]

        raw_landed = [[sem(f"raw_landed{p}{j}") for j in range(3)] for p in range(2)]
        hi_ready = sem("hi_ready")
        lo_ready = sem("lo_ready")
        split_used = sem("split_used")
        x_loaded = sem("x_loaded")
        consts_loaded = sem("consts_loaded")
        gain_loaded = sem("gain_loaded")
        x_ready = sem("x_ready")
        squares_ready = sem("squares_ready")
        xn_ready = sem("xn_ready")
        tr_ready = sem("tr_ready")
        hhi_ready = sem("hhi_ready")
        hlo_ready = sem("hlo_ready")
        th_ready = sem("th_ready")
        sg_ready = sem("sg_ready")
        actf_ready = sem("actf_ready")
        acthi_ready = sem("acthi_ready")
        actlo_ready = sem("actlo_ready")
        y_ready = sem("y_ready")
        dve_step = sem("dve_step")
        ne2_ready = sem("ne2_ready")
        f2_ready = sem("f2_ready")
        ln2_ready = sem("ln2_ready")
        b2_ready = sem("b2_ready")
        t2_ready = sem("t2_ready")
        ex2_ready = sem("ex2_ready")
        dec2_ready = sem("dec2_ready")
        dir_ready = sem("dir_ready")
        lbe_ready = sem("lbe_ready")
        lb_ready = sem("lb_ready")
        neq_ready = sem("neq_ready")
        q2_ready = sem("q2_ready")
        v2_ready = sem("v2_ready")
        aq2_ready = sem("aq2_ready")
        hgth_ready = sem("hgth_ready")
        gg2_ready = sem("gg2_ready")
        zero_ready = sem("zero_ready")
        kh1_ready = sem("kh1_ready")
        kst_ready = sem("kst_ready")
        ksr_ready = sem("ksr_ready")
        asc2_ready = sem("asc2_ready")
        aT2_ready = sem("aT2_ready")
        kvp_ready = sem("kvp_ready")
        state_ready = sem("state_ready")
        inter_used = sem("inter_used")
        o2_ready = sem("o2_ready")
        osq_ready = sem("osq_ready")
        yh_ready = sem("yh_ready")
        gate_th_ready = sem("gate_th_ready")
        gate_ready = sem("gate_ready")
        asq_ready = sem("asq_ready")
        aqk_ready = sem("aqk_ready")
        atr_ready = sem("atr_ready")
        aT_ready = sem("aT_ready")
        as_ready = sem("as_ready")
        amax_ready = sem("amax_ready")
        aexp_ready = sem("aexp_ready")
        aptr_ready = sem("aptr_ready")
        apT_ready = sem("apT_ready")
        apv_ready = sem("apv_ready")
        ya_ready = sem("ya_ready")
        br_ready = sem("br_ready")
        merged_ready = sem("merged_ready")
        m2_loaded = sem("m2_loaded")
        late_loaded = sem("late_loaded")
        angles_ready = sem("angles_ready")
        sines_ready = sem("sines_ready")
        gains_used = sem("gains_used")
        mgain_loaded = sem("mgain_loaded")
        b4_ready = sem("b4_ready")
        b4sq_ready = sem("b4sq_ready")
        latn_ready = sem("latn_ready")
        lattr_ready = sem("lattr_ready")
        lathi_ready = sem("lathi_ready")
        latlo_ready = sem("latlo_ready")
        rowsq_ready = sem("rowsq_ready")
        rowsk_ready = sem("rowsk_ready")
        v_ready = sem("v_ready")
        gth_ready = sem("gth_ready")
        gg_ready = sem("gg_ready")
        rtr_ready = sem("rtr_ready")
        qkT_ready = sem("qkT_ready")
        rsc_ready = sem("rsc_ready")
        scT_ready = sem("scT_ready")
        yr_ready = sem("yr_ready")
        yrsq_ready = sem("yrsq_ready")
        yret_ready = sem("yret_ready")
        q_ready = sem("q_ready")
        qsq_ready = sem("qsq_ready")
        kv_ready = sem("kv_ready")
        ksq_ready = sem("ksq_ready")
        qf_ready = sem("qf_ready")
        kf_ready = sem("kf_ready")
        mtr_ready = sem("mtr_ready")
        mT_ready = sem("mT_ready")
        msc_ready = sem("msc_ready")
        masked_ready = sem("masked_ready")
        negmax_ready = sem("negmax_ready")
        exp_ready = sem("exp_ready")
        ptr_ready = sem("ptr_ready")
        pT_ready = sem("pT_ready")
        pv_ready = sem("pv_ready")
        ymla_ready = sem("ymla_ready")
        stored = sem("stored")
        route_loaded = sem("route_loaded")
        logits_done = sem("logits_done")
        glogits_ready = sem("glogits_ready")
        gexp_ready = sem("gexp_ready")
        elogits_ready = sem("elogits_ready")
        eexp_ready = sem("eexp_ready")
        picks_ready = sem("picks_ready")
        counts_done = sem("counts_done")
        diag_ready = sem("diag_ready")
        rows_done = sem("rows_done")
        rows_ready = sem("rows_ready")
        cum_ready = sem("cum_ready")
        gu_landed = [sem(f"gu_landed{e}") for e in range(RING)]
        down_landed = [sem(f"down_landed{e}") for e in range(RING)]
        acc_open = sem("acc_open")
        take_step = sem("take_step")
        take_ready = sem("take_ready")
        gathered = sem("gathered")
        he_ready = sem("he_ready")
        gu_done = sem("gu_done")
        gu_copied = sem("gu_copied")
        turned = sem("turned")
        eth_ready = sem("eth_ready")
        esg_ready = sem("esg_ready")
        ehid_ready = sem("ehid_ready")
        ydown_done = sem("ydown_done")
        y_copied = sem("y_copied")
        give_step = sem("give_step")
        give_ready = sem("give_ready")
        given = sem("given")

        OPEN = 1

        plan = []
        b0, m0 = 0, SLOTS - 1
        moe = stages[-1][0] == "moe"
        for st in stages[:-1] if moe else stages:
            nb = {"ffn": BATCH_FFN, "mid": BATCH_MID, "mix2": BATCH_MIX2}[st[0]]
            plan.append((st, b0, m0))
            b0, m0 = b0 + nb, m0 + 6 * nb

        def batches(i):
            return {"ffn": BATCH_FFN, "mid": BATCH_MID, "mix2": BATCH_MIX2}[plan[i][0][0]]

        def halves(d):
            return [(0, GC // 2), (GC // 2, GC)][::-1 if d else 1]

        def layer(st):
            return 0 if st[0] in ("mix2", "moe") else st[1]

        def kind_index(i):
            return sum(plan[k][0][0] == plan[i][0][0] for k in range(i))

        def columns_index(i):
            return sum({"ffn": 1, "mid": 2, "mix2": 3}[plan[k][0][0]] for k in range(i))

        def first4(m):
            return [m - 5, m - 4, m - 2, m - 1]

        def mid_pos(i, job, half):
            m, n = plan[i][2], 3 * batches(i)
            if job < 2:
                return first4(m)[2 * half + job]
            if (job, half) == (n - 1, 1):
                return m + 2 * n - 3
            return m + 2 * (job - 2) + half

        def mid_order(i, o):
            n = 3 * batches(i)
            tail = {2 * n - 5: (0, 0, True), 2 * n - 4: (1, 0, True), 2 * n - 3: (n - 1, 1, False),
                    2 * n - 2: (0, 1, True), 2 * n - 1: (1, 1, True)}
            return tail.get(o, (2 + o // 2, o % 2, False))

        def mid_jobs(l):
            w, uq, ukv, wo = a["w_in"], a["w_uq"], a["w_ukv"], a["w_o"]
            jobs = []
            for c0, n in [(2048, CB)] + [(c * 512, 512) for c in range(4)]:
                for k in range(2):
                    jobs.append((w[l, k * 512:(k + 1) * 512, c0:c0 + n].rearrange("(k p) n -> p k n", p=P), 2 * n))
            for k in range(2):
                jobs.append((uq[l, k * P:(k + 1) * P, :], LAT))
            for k in range(2):
                jobs.append((ukv[l, :, k * 512:(k + 1) * 512], S))
            for c in range(2):
                for k in range(2):
                    jobs.append((wo[l, k * 512:(k + 1) * 512, c * 512:(c + 1) * 512].rearrange("(k p) n -> p k n", p=P), HALF))
            return jobs

        def mix2_jobs():
            w, wa, wh, wo = (a[n + "_2"] for n in ("w_in", "w_attn_branch", "w_hgrn_branch", "w_out"))
            jobs = []
            for c0, n in [(1280, 512), (1792, 512), (768, 512), (2304, 512), (0, 512), (512, 256), (2816, 512),
                          (3328, 512), (3840, 512), (4352, 512), (4864, 512)]:
                for k in range(2):
                    jobs.append((w[0, k * 512:(k + 1) * 512, c0:c0 + n].rearrange("(k p) n -> p k n", p=P), 2 * n))
            for ww in (wa, wh):
                for c in range(2):
                    jobs.append((ww[0, :, c * 512:(c + 1) * 512].rearrange("(k p) n -> p k n", p=P), HALF))
            for c in range(2):
                for k in range(2):
                    jobs.append((wo[0, k * 512:(k + 1) * 512, c * 512:(c + 1) * 512].rearrange("(k p) n -> p k n", p=P), HALF))
            return jobs

        def last_use(i, k):
            st, b, m = plan[i]
            if st[0] != "ffn":
                return [mid_pos(i, 3 * k + j, 1) + 1 for j in range(3)]
            f4 = first4(m)
            g, u = (f4[2], f4[3]) if k == 0 else (m + 3 * (2 * k - 1) + 1, m + 3 * (2 * k - 1) + 2)
            return g + 1, u + 1, m + 3 * (2 * k + 1) + 1

        def landed_view(par, st, job, half):
            r = raw[:, par, job % 3, :]
            if st[0] == "ffn":
                if job < 2:
                    return r.rearrange("p (k f) -> p k f", f=2 * P)[:, :, half * P:(half + 1) * P]
                return r[:, half * HALF:(half + 1) * HALF]
            n = (MID_HALF if st[0] == "mid" else MIX2_HALF)[job]
            return r[:, half * n:(half + 1) * n]

        MID_HALF = [n for _, n in mid_jobs(0)]
        MIX2_HALF = [n for _, n in mix2_jobs()] if "w_in_2" in a else None

        def slot_view(t, m, like):
            n = t[:, m % SLOTS, :]
            if len(like.shape) == 3:
                return n.rearrange("p (k f) -> p k f", f=like.shape[2])
            return n[:, 0:like.shape[1]]

        def batch_value(b, r):
            return (b // 2 + 1) * 16 + r * 16

        block = ctx.enter_context(nc.Block())

        @block.sync
        def _(sp):
            sp.dma_start(x[:], a["x"][0].rearrange("(t p) d -> p t d", p=P)).then_inc(x_loaded, 16)
            sp.dma_start(ident[:], a["ident"]).then_inc(x_loaded, 16)

            def load_constants():
                sp.dma_start(pos_i[:], a["positions"]).then_inc(consts_loaded, 16)
                sp.dma_start(freq[:], a["freq"]).then_inc(consts_loaded, 16)
                sp.dma_start(decay[:], a["decay"]).then_inc(consts_loaded, 16)
                sp.dma_start(causal[:], a["causal"]).then_inc(consts_loaded, 16)

            def ffn_batch(i, par, cols, wait):
                _, l, n = plan[i][0]
                wg, wu, wd = (a[f"ffn{n}_w_{w}"] for w in ("gate", "up", "down"))
                for j in range(3):
                    if wait is not None:
                        sp.wait_ge(lo_ready, wait[j])
                    if j < 2:
                        src = (wg, wu)[j][l, :, bass.ds(cols * 2 * P, 2 * P)].rearrange("(k p) f -> p k f", p=P)
                        dst = raw[:, par, j, :].rearrange("p (k f) -> p k f", f=2 * P)
                    else:
                        src = wd[l, bass.ds(cols * 2 * P, 2 * P), :].rearrange("(h p) n -> p h n", p=P)
                        dst = raw[:, par, j, :].rearrange("p (h n) -> p h n", n=D)
                    sp.dma_start(dst, src).then_inc(raw_landed[par][j], 16)

            def mid_batch(i, k, wait):
                par = (plan[i][1] + k) % 2
                for j in range(3):
                    if wait is not None:
                        sp.wait_ge(lo_ready, wait[j])
                    src, n = (mid_jobs(plan[i][0][1]) if plan[i][0][0] == "mid" else mix2_jobs())[3 * k + j]
                    dst = raw[:, par, j, 0:2 * n]
                    if len(src.shape) == 3:
                        dst = dst.rearrange("p (k n) -> p k n", n=src.shape[2])
                    sp.dma_start(dst, src).then_inc(raw_landed[par][j], 16)

            for i, (st, b, m) in enumerate(plan):
                before = [None if i == 0 else last_use(i - 1, batches(i - 1) - 2 + k) for k in range(2)]
                if st[0] == "ffn":
                    for k in range(2):
                        ffn_batch(i, (b + k) % 2, k, before[k])
                        if i == k == 0:
                            load_constants()
                    ffn_batch(i, b % 2, 2, last_use(i, 0))
                    with sp.Fori(0, 4) as r:
                        for k in range(2):
                            ffn_batch(i, (b + 3 + k) % 2, r * 2 + (3 + k), [w + r * 12 for w in last_use(i, k + 1)])
                else:
                    for k in range(batches(i)):
                        mid_batch(i, k, before[k] if k < 2 else last_use(i, k - 2))
                        if i == k == 0:
                            load_constants()

            def expert(e, j, used):
                for w, name in enumerate(("gate", "up", "down")):
                    src = a[f"w_exp_{name}_2"][0, bass.ds(e, 1)].rearrange("e (p k) n -> p (e k n)", p=P)
                    if w == 0 and used is not None:
                        sp.wait_ge(gu_done, used * 2)
                    if w == 2 and used is not None:
                        sp.wait_ge(ydown_done, used * 2)
                    sp.dma_start(expert_w[j][w][:], src).then_inc(gu_landed[j] if w < 2 else down_landed[j], 16)

            if moe:
                last = len(plan) - 1
                if plan:
                    for k in range(2):
                        for w in last_use(last, batches(last) - 2 + k):
                            sp.wait_ge(lo_ready, w)
                expert(0, 0, None)
                sp.wait_ge(tr_ready, 4 * columns_index(last) + 12)
                expert(2, 2, None)
                sp.wait_ge(x_ready, 4 * last + 4)
                expert(1, 1, None)
                sp.wait_ge(cum_ready, 1)
                with sp.Fori(0, NE // RING - 1) as r:
                    for j in range(RING):
                        expert(r * RING + (RING + j), j, sp.value_load(cum[0:1, bass.ds(r * RING + (j + 1), 1)],
                                                                       min_val=1, max_val=MAXB))
                for e in range(NE // RING * RING, NE):
                    expert(e, e % RING, sp.value_load(cum[0:1, e - RING + 1:e - RING + 2], min_val=1, max_val=MAXB))
            sp.wait_ge(x_ready, 4 * len(stages))
            sp.dma_start(out[0].rearrange("(t p) d -> p t d", p=P), x[:]).then_inc(stored, 16)
            sp.wait_ge(stored, 16)

        @block.gpsimd
        def _(gp):
            last_mid = None
            for i, (st, b, m) in enumerate(plan):
                name = {"ffn": f"ffn{st[-1]}_norm", "mid": "mix_norm", "mix2": "g_mix_2"}[st[0]]
                if i:
                    gp.wait_ge(xn_ready, 2 * i)
                gp.dma_start(gain[:], a[name][layer(st):layer(st) + 1, :].broadcast_to([P, D])).then_inc(gain_loaded, 16)
                if st[0] == "mix2":
                    gp.wait_ge(xn_ready, 2 * i + 2)
                    for dst, src in [(axial[:], a["axial"]), (lb_in[:], a["lb_cols"]),
                                     (g_hn[:], a["hgrn_norm_2"][0:1, :].broadcast_to([P, GD]))]:
                        gp.dma_start(dst, src).then_inc(m2_loaded, 16)
                    gp.wait_ge(tr_ready, 4 * columns_index(i) + 4)
                    for dst, src in [(carry[:], a["carry"]), (reach[:], a["reach"])]:
                        gp.dma_start(dst, src).then_inc(late_loaded, 16)
                    for d in range(2):
                        nc.gpsimd.memset(g_aT[d][:], 0.0).then_inc(zero_ready, 1)
                    gp.wait_ge(t2_ready, 4)
                    for e, src in enumerate((a["q_norm_2"], a["k_norm_2"])):
                        gp.dma_start(g_64[:, e, :], src[0:1, :].broadcast_to([P, AD])).then_inc(late_loaded, 16)
                if st[0] == "mid":
                    if last_mid is not None:
                        gp.wait_ge(x_ready, 4 * last_mid + 4)
                    last_mid = i
                    l = st[1]
                    for dst, src in [
                        (g_ret[:], a["ret_head_norm"][l:l + 1].rearrange("a h d -> a (h d)")),
                        (g_lat[:, 0:S], a["q_lat_norm"][l:l + 1, :]), (g_lat[:, S:LAT], a["kv_lat_norm"][l:l + 1, :]),
                        (g_q[:, 0:NOPE], a["qn_nope"][l:l + 1, :]), (g_q[:, NOPE:QD], a["qn_rope"][l:l + 1, :]),
                        (g_k[:, 0:NOPE], a["kn_nope"][l:l + 1, :]), (g_k[:, NOPE:QD], a["kn_rope"][l:l + 1, :]),
                    ]:
                        gp.dma_start(dst, src.broadcast_to([P, dst.shape[1]])).then_inc(mgain_loaded, 16)

            if moe:
                i = len(plan)
                gp.wait_ge(aqk_ready, 2)
                gp.dma_start(gain[:], a["g_ffn_2"][0:1, :].broadcast_to([P, D])).then_inc(gain_loaded, 16)
                gp.wait_ge(ya_ready, 2)
                for dst, src in [
                    (w_group[:], a["w_router_group_2"][0].rearrange("(p k) n -> p k n", p=P)),
                    (w_router[:], a["w_router_expert_2"][0].rearrange("(p k) n -> p k n", p=P)),
                    (b_router[:, 0:NG], a["b_router_group_2"][0:1, :].broadcast_to([P, NG])),
                    (b_router[:, NG:], a["b_router_expert_2"][0:1, :].broadcast_to([P, NE])),
                    (route[:], a["route"]), (square[:], a["square"]),
                ]:
                    gp.dma_start(dst, src).then_inc(route_loaded, 16)

        @block.scalar
        def _(act):
            def split_hi(st, par, value, job, half, m, slot, inc=1):
                act.wait_ge(raw_landed[par][job % 3], value)
                if not (isinstance(m, int) and m < SLOTS):
                    act.wait_ge(split_used, OPEN + m - (SLOTS - 1))
                src = landed_view(par, st, job, half)
                nc.scalar.activation(slot_view(whi, slot, src), src, ACT.Copy).then_inc(hi_ready, inc)

            def columns(n):
                for g in range(4):
                    t, h = g // 2, g % 2
                    act.wait_ge(tr_ready, 4 * n + g + 1)
                    nc.scalar.activation(hhi[:, 4 * h:4 * h + 4, t * P:(t + 1) * P],
                                         TR[g][:].rearrange("p (k c) -> p k c", c=P),
                                         ACT.Copy).then_inc(hhi_ready, 1)

            def first_splits(i):
                st, b, m = plan[i]
                for o, (job, half) in enumerate([(0, 0), (1, 0), (0, 1), (1, 1)]):
                    split_hi(st, b % 2, batch_value(b, 0), job, half, first4(m)[o], first4(m)[o], 2 if o == 1 else 1)

            def ffn(i):
                st, b, m = plan[i]
                base = 22 * kind_index(i)

                def window(c, o, r, last=False):
                    tail = last and i + 1 == len(plan)
                    k = o // 2
                    act.wait_ge(split_used, OPEN + m - 3 + 3 * c)
                    nc.scalar.activation(th[:, o % 2, :], GU[o % 2][:, 0:S], ACT.Tanh, scale=0.5).then_inc(th_ready, 1)
                    split_hi(st, (b + k) % 2, batch_value(b + k, r), 2, o % 2, m + 3 * c, m + 3 * o, 3 if tail else 1)
                    act.wait_ge(actf_ready, base + c + 1)
                    nc.scalar.activation(act_hi[:, o % 2, :], act_f[:, o % 2, :], ACT.Copy).then_inc(acthi_ready, 1)
                    if tail:
                        return
                    for j in range(2):
                        split_hi(plan[i + 1][0] if last else st, (b + k + 1) % 2, batch_value(b + k + 1, r),
                                 j, o % 2, m + 3 * c + 1 + j, m + 3 * o + 1 + j)

                with act.Fori(0, 5) as r:
                    for o in range(4):
                        window(r * 4 + o, o, r)
                for o in (20, 21):
                    window(o, o, 0, last=True)

            def splitter(i):
                st, b, m = plan[i]
                done = [0]

                def splits(upto):
                    for o in range(done[0], upto + 1):
                        job, half, nxt = mid_order(i, o)
                        bb = b + batches(i) if nxt else b + job // 3
                        tail = i + 1 == len(plan)
                        if not (nxt and tail):
                            inc = 3 if tail and (job, half) == (3 * batches(i) - 1, 0) else 1
                            split_hi(plan[i + 1][0] if nxt else st, bb % 2, batch_value(bb, 0), job, half, m + o, m + o, inc)
                    done[0] = upto + 1
                return splits

            def mixer(i):
                st, b, m = plan[i]
                z = kind_index(i)
                splits = splitter(i)

                splits(5)
                act.wait_ge(split_used, OPEN + mid_pos(i, 1, 1) + 1)
                for t in range(T):
                    nc.scalar.activation(b4[:, t, :], bank[t][:, 0:CB], ACT.Copy).then_inc(b4_ready, 1)
                for t in range(T):
                    nc.scalar.activation(sq[:, t, 0:CB], bank[t][:, 0:CB], ACT.Square).then_inc(b4sq_ready, 1)
                splits(9)
                for t in range(T):
                    act.wait_ge(lattr_ready, 2 * z + t + 1)
                    nc.scalar.activation(lat_hi[:, :, t * P:(t + 1) * P],
                                         bank[6 + t][:, 0:LAT].rearrange("p (k c) -> p k c", c=P),
                                         ACT.Copy).then_inc(lathi_ready, 1)
                splits(13)
                act.wait_ge(split_used, OPEN + mid_pos(i, 7, 1) + 1)
                for t in range(T):
                    nc.scalar.activation(v[:, t, :], bank[2 + t][:], ACT.Copy).then_inc(v_ready, 1)
                splits(17)
                act.wait_ge(split_used, OPEN + mid_pos(i, 9, 1) + 1)
                for t in range(T):
                    nc.scalar.activation(gg[:, t, :], bank[t][:], ACT.Tanh, scale=0.5).then_inc(gth_ready, 1)
                splits(21)
                for g in range(4):
                    act.wait_ge(rtr_ready, 4 * z + g + 1)
                    o, t = g // 2, g % 2
                    nc.scalar.activation(qkT[:, o, :, t * P:(t + 1) * P],
                                         bank[4 + g][:].rearrange("p (h c) -> p h c", c=P),
                                         ACT.Copy).then_inc(qkT_ready, 1)
                act.wait_ge(split_used, OPEN + mid_pos(i, 11, 1) + 1)
                for g in range(4):
                    t, h = g // 2, g % 2
                    nc.scalar.activation(q[:, t, h * LAT:(h + 1) * LAT], bank[g][:, 0:LAT], ACT.Copy).then_inc(q_ready, 1)
                splits(23)
                act.wait_ge(q_ready, 4 * z + 4)
                for t in range(T):
                    nc.scalar.activation(sqq[:, t, :], q[:, t, :], ACT.Square).then_inc(qsq_ready, 1)
                splits(25)
                act.wait_ge(split_used, OPEN + mid_pos(i, 13, 1) + 1)
                for g in range(4):
                    t, h = g // 2, g % 2
                    nc.scalar.activation(kvs[:, t, h * 512:(h + 1) * 512], bank[g][:], ACT.Copy).then_inc(kv_ready, 1)
                for t in range(T):
                    act.wait_ge(yr_ready, 2 * z + t + 1)
                    nc.scalar.activation(sq[:, t, 0:512], bank[4 + t][:], ACT.Square).then_inc(yrsq_ready, 1)
                act.wait_ge(kv_ready, 4 * z + 4)
                for t in range(T):
                    nc.scalar.activation(sqk[:, t, :].rearrange("p (h c) -> p h c", c=NOPE),
                                         kvs[:, t, :].rearrange("p (h c) -> p h c", c=P)[:, :, 0:NOPE],
                                         ACT.Square).then_inc(ksq_ready, 1)
                splits(29)
                for g in range(8):
                    act.wait_ge(mtr_ready, 8 * z + g + 1)
                    o, t, hh = g // 4, g // 2 % 2, g % 2
                    nc.scalar.activation((qfT, kfT)[o][0:QD, 4 * hh:4 * hh + 4, t * P:(t + 1) * P],
                                         bank[4 + g % 4][0:QD, :].rearrange("p (h c) -> p h c", c=P),
                                         ACT.Copy).then_inc(mT_ready, 1)
                act.wait_ge(negmax_ready, z + 1)
                for h in range(MH):
                    for t in range(T):
                        w = slice(0, P) if t == 0 else slice(P, 3 * P)
                        nc.scalar.activation(prob[:, h, w], prob[:, h, w], ACT.Exp, scale=MLA_SCALE,
                                             bias=small[:, 2, 2 * h + t:2 * h + t + 1],
                                             accum_out=sums[:, 0, h, t:t + 1]).then_inc(exp_ready, 1)
                columns(columns_index(i) + 1)
                splits(35)

            def mixer2(i):
                st, b, m = plan[i]
                splits = splitter(i)

                def product(job):
                    act.wait_ge(split_used, OPEN + mid_pos(i, job, 1) + 1)

                def decays(d):
                    for h in range(GH):
                        nc.scalar.activation(g_ee[d][:, h, :], bank[4 * d + h][:, 0:S], ACT.Exp, scale=-1.0).then_inc(ne2_ready, 1)

                def factors(d):
                    act.wait_ge(t2_ready, 2 * d + 1)
                    if d:
                        act.wait_ge(asc2_ready, 2)
                    nc.scalar.activation(g_qh[:], g_t[:], ACT.Exp).then_inc(ex2_ready, 1)
                    nc.scalar.activation(g_kh[:], g_t[:], ACT.Exp, scale=-1.0).then_inc(ex2_ready, 1)
                    nc.scalar.activation(g_qi[d][:], g_b[:], ACT.Exp).then_inc(ex2_ready, 1)
                    last = GC - 1 if d == 0 else 0
                    nc.scalar.activation(dec[:, d, :, :], g_b[:].rearrange("p h (n c) -> p h n c", c=GC)[:, :, :, last],
                                         ACT.Exp).then_inc(dec2_ready, 1)
                    act.wait_ge(t2_ready, 2 * d + 2)
                    nc.scalar.activation(g_ks[:], g_ee[d][:], ACT.Exp).then_inc(ex2_ready, 1)

                def gates(c):
                    product(15 + 2 * c)
                    for t in range(T):
                        nc.scalar.activation(gate[c][:, t, :], bank[6 + t][:], ACT.Tanh, scale=0.5).then_inc(gate_th_ready, 1)

                def state_rows(d):
                    for t in range(T):
                        act.wait_ge(kst_ready, 2 * d + t + 1)
                        nc.scalar.activation(g_ksr[d][:, t, :], bank[2 + t][:], ACT.Copy).then_inc(ksr_ready, 1)

                nc.scalar.preload_act_table_set("natural_log_exp_and_others")
                act.wait_ge(lb_ready, 1)
                nc.scalar.activation(lb[:, 1, :, :], lb[:, 0, :, :], ACT.Exp).then_inc(lbe_ready, 1)
                splits(5)
                product(1)
                decays(0)
                act.wait_ge(f2_ready, 1)
                nc.scalar.activation(g_ee[0][:], g_b[:], ACT.Ln).then_inc(ln2_ready, 1)
                splits(9)
                product(3)
                decays(1)
                splits(13)
                product(5)
                for h in range(GH):
                    nc.scalar.activation(g_q2[:, h, :], bank[h][:, 0:S], ACT.Exp, scale=-1.0).then_inc(neq_ready, 1)
                factors(0)
                splits(17)
                product(7)
                for t in range(T):
                    nc.scalar.activation(g_v[:, t, :], bank[4 + t][:], ACT.Copy).then_inc(v2_ready, 1)
                splits(21)
                product(9)
                for t in range(T):
                    nc.scalar.activation(aqkv[:, t, 0:512], bank[6 + t][:], ACT.Copy).then_inc(aq2_ready, 1)
                act.wait_ge(f2_ready, 2)
                nc.scalar.activation(g_ee[1][:], g_b[:], ACT.Ln).then_inc(ln2_ready, 1)
                splits(25)
                product(11)
                for t in range(T):
                    nc.scalar.activation(aqkv[:, t, 512:768], bank[4 + t][:, 0:S], ACT.Copy).then_inc(aq2_ready, 1)
                splits(29)
                nc.scalar.preload_act_table(ACT.Tanh)
                product(13)
                for t in range(T):
                    nc.scalar.activation(g_g[:, t, :], bank[6 + t][:], ACT.Tanh, scale=0.5).then_inc(hgth_ready, 1)
                state_rows(0)
                factors(1)
                act.wait_ge(dir_ready, 8)
                gates(0)
                splits(33)
                state_rows(1)
                gates(1)
                for t in range(T):
                    nc.scalar.activation(a_sq[:, t, :], aqkv[:, t, 0:640], ACT.Square).then_inc(asq_ready, 1)
                splits(37)
                gates(2)
                splits(41)
                act.wait_ge(o2_ready, 1)
                for t in range(T):
                    nc.scalar.activation(h_sq[:, t, :], bank[t][:], ACT.Square).then_inc(osq_ready, 1)
                for g in range(6):
                    t, e = divmod(g, 3)
                    act.wait_ge(atr_ready, g + 1)
                    n = 4 if e < 2 else 2
                    dst = aT_q[0:AD, 4 * e:4 * e + 4, t * P:(t + 1) * P] if e < 2 else aT_k[0:AD, :, t * P:(t + 1) * P]
                    nc.scalar.activation(dst, bank[2 + g % 4][0:AD, 0:n * P].rearrange("p (h c) -> p h c", c=P),
                                         ACT.Copy).then_inc(aT_ready, 1)
                gates(3)
                splits(45)
                for G in range(AKV):
                    act.wait_ge(amax_ready, G + 1)
                    if G:
                        act.wait_ge(aptr_ready, 4)
                    for h in range(4):
                        for t in range(T):
                            c = 8 * G + 2 * h + t
                            nc.scalar.activation(a_pr[:, h, t, :], bank[2 + h][:, t * S:(t + 1) * S], ACT.Exp, scale=AD ** -0.5,
                                                 bias=small[:, 2, c:c + 1],
                                                 accum_out=sums[:, 0, 4 * G + h, t:t + 1]).then_inc(aexp_ready, 1)
                columns(columns_index(i) + 1)
                splits(53)
                columns(columns_index(i) + 2)
                splits(59)

            def norm_squares(i):
                for t in range(T):
                    if i == 0:
                        act.wait_ge(x_loaded, 32)
                    else:
                        act.wait_ge(x_ready, 4 * i + 2 * t - 2)
                    nc.scalar.activation(xn[:, t, :], x[:, t, :], ACT.Square,
                                         accum_out=small[:, 0, t:t + 1]).then_inc(squares_ready, 1)

            def experts(i):
                n = columns_index(i)
                for g in range(4):
                    t, h = g // 2, g % 2
                    act.wait_ge(tr_ready, 4 * n + g + 1)
                    nc.scalar.activation(hcol[:, 4 * h:4 * h + 4, t * P:(t + 1) * P],
                                         TR[g][:].rearrange("p (k c) -> p k c", c=P), ACT.Copy).then_inc(hhi_ready, 1)
                act.wait_ge(glogits_ready, 1)
                nc.scalar.activation(g4[:, :, 1, :], g4[:, :, 0, :], ACT.Exp).then_inc(gexp_ready, 1)
                act.wait_ge(elogits_ready, 1)
                nc.scalar.activation(x8[:, :, 1, :], x8[:, :, 0, :], ACT.Exp).then_inc(eexp_ready, 1)
                act.wait_ge(rows_done, 1)
                for h in range(2):
                    nc.scalar.activation(rows4[:, 2 * h:2 * h + 2, :].rearrange("p v c -> p (v c)"), bank[6 + h][:],
                                         ACT.Copy).then_inc(rows_ready, 1)
                act.wait_ge(gathered, 1)
                nc.scalar.activation(h_e[:].rearrange("p k s -> p (k s)"), bank[6][:, 0:KC * BS], ACT.Copy).then_inc(he_ready, 1)
                act.wait_ge(cum_ready, 1)
                total = act.value_load(cum[0:1, NE:NE + 1], min_val=NE, max_val=MAXB)
                with act.Fori(0, total) as k:
                    act.wait_ge(gu_done, k * 2 + 1)
                    nc.scalar.activation(gu_sb[:, 0, :], GU[0][:], ACT.Copy).then_inc(gu_copied, 1)
                    act.wait_ge(turned, k + 1)
                    nc.scalar.activation(e_th[:].rearrange("p c s -> p (c s)"), bank[7][:, 0:FK * BS], ACT.Tanh,
                                         scale=0.5).then_inc(eth_ready, 1)
                    act.wait_ge(gathered, k + 2)
                    nc.scalar.activation(h_e[:].rearrange("p k s -> p (k s)"), bank[6][:, 0:KC * BS],
                                         ACT.Copy).then_inc(he_ready, 1)
                    act.wait_ge(ydown_done, k * 2 + 1)
                    nc.scalar.activation(y_sb[:, 0:512], GU[0][:], ACT.Copy).then_inc(y_copied, 1)

            def sines():
                nc.scalar.preload_act_table(ACT.Sin)
                act.wait_ge(angles_ready, 1)
                nc.scalar.activation(turns[:], ang[:], ACT.Sin, scale=0.5).then_inc(sines_ready, 1)
                for (s_, n0, n1) in ((sin_r, 0, RD // 2), (sin_m, RD // 2, NF)):
                    nc.scalar.activation(s_[:], ang[:, :, n0:n1], ACT.Sin).then_inc(sines_ready, 1)
                nc.scalar.preload_act_table(ACT.Tanh)

            nc.scalar.preload_act_table(ACT.Tanh)
            for i, (st, b, m) in enumerate(plan):
                norm_squares(i)
                if i == 0:
                    first_splits(0)
                columns(columns_index(i))
                if i == 0:
                    sines()
                {"ffn": ffn, "mid": mixer, "mix2": mixer2}[st[0]](i)
            if moe:
                norm_squares(len(plan))
                experts(len(plan))

        @block.vector
        def _(dve):
            steps = [0]

            def link(*ins):
                for step in ins:
                    steps[0] += 1
                    step.then_inc(dve_step, 1)
                dve.wait_ge(dve_step, steps[0])

            def split_lo(st, par, job, half, m, slot, inc=1):
                dve.wait_ge(hi_ready, m + 1)
                src = landed_view(par, st, job, half)
                nc.vector.tensor_tensor(slot_view(wlo, slot, src), src,
                                        slot_view(whi, slot, src).bitcast(F32), ALU.subtract).then_inc(lo_ready, inc)

            def first_splits(i):
                st, b, m = plan[i]
                for o, (job, half) in enumerate([(0, 0), (1, 0), (0, 1), (1, 1)]):
                    split_lo(st, b % 2, job, half, first4(m)[o], first4(m)[o], 2 if o == 1 else 1)

            def rsqrt(w, y):
                h, o = small[:, 1, 0:w], small[:, 4, 0:w]
                link(nc.vector.tensor_scalar(o.bitcast(I32), h.bitcast(I32), 1, None, ALU.logical_shift_right))
                link(nc.vector.tensor_scalar(y.bitcast(I32), o.bitcast(I32), -1.0, float(0x5f3759df), ALU.mult, ALU.add))
                for _ in range(3):
                    link(nc.vector.tensor_tensor(o, y, y, ALU.mult))
                    link(nc.vector.scalar_tensor_tensor(o, o, -0.5, h, ALU.mult, ALU.mult))
                    link(nc.vector.scalar_tensor_tensor(y, o, 1.5, y, ALU.add, ALU.mult))

            def mean_eps(c0, c1, n):
                return nc.vector.tensor_scalar(small[:, 1, c0:c1], small[:, 0, c0:c1], 1.0 / n, EPS, ALU.mult, ALU.add)

            def columns(n):
                for g in range(4):
                    t, h = g // 2, g % 2
                    dve.wait_ge(hhi_ready, 4 * n + g + 1)
                    nc.vector.tensor_tensor(hlo[:, 4 * h:4 * h + 4, t * P:(t + 1) * P],
                                            TR[g][:].rearrange("p (k c) -> p k c", c=P),
                                            hhi[:, 4 * h:4 * h + 4, t * P:(t + 1) * P].bitcast(F32),
                                            ALU.subtract).then_inc(hlo_ready, 1)

            def update_x(i, scale):
                dve.wait_ge(y_ready, i + 1)
                for t in range(T):
                    for h in range(2):
                        nc.vector.scalar_tensor_tensor(x[:, t, h * 512:(h + 1) * 512], Y[2 * t + h][:], scale,
                                                       x[:, t, h * 512:(h + 1) * 512],
                                                       ALU.mult, ALU.add).then_inc(x_ready, 1)

            def ffn(i):
                st, b, m = plan[i]
                base = 22 * kind_index(i)

                def window(c, o, last=False):
                    tail = last and i + 1 == len(plan)
                    k = o // 2
                    dve.wait_ge(th_ready, base + c + 1)
                    nc.vector.scalar_tensor_tensor(sg[:, o % 2, :], th[:, o % 2, :], 1.0, GU[o % 2][:, 0:S],
                                                   ALU.add, ALU.mult).then_inc(sg_ready, 1)
                    dve.wait_ge(sg_ready, base + c + 1)
                    nc.vector.tensor_tensor(act_f[:, o % 2, :], sg[:, o % 2, :], GU[o % 2][:, S:2 * S],
                                            ALU.mult).then_inc(actf_ready, 1)
                    split_lo(st, (b + k) % 2, 2, o % 2, m + 3 * c, m + 3 * o, 3 if tail else 1)
                    dve.wait_ge(acthi_ready, base + c + 1)
                    nc.vector.tensor_tensor(act_lo[:, o % 2, :], act_f[:, o % 2, :],
                                            act_hi[:, o % 2, :].bitcast(F32), ALU.subtract).then_inc(actlo_ready, 1)
                    if tail:
                        return
                    for j in range(2):
                        split_lo(plan[i + 1][0] if last else st, (b + k + 1) % 2, j, o % 2,
                                 m + 3 * c + 1 + j, m + 3 * o + 1 + j)

                with dve.Fori(0, 5) as r:
                    for o in range(4):
                        window(r * 4 + o, o)
                for o in (20, 21):
                    window(o, o, last=True)
                update_x(i, 0.25)

            def splitter(i):
                st, b, m = plan[i]
                done = [0]

                def splits(upto):
                    for o in range(done[0], upto + 1):
                        job, half, nxt = mid_order(i, o)
                        bb = b + batches(i) if nxt else b + job // 3
                        tail = i + 1 == len(plan)
                        if not (nxt and tail):
                            inc = 3 if tail and (job, half) == (3 * batches(i) - 1, 0) else 1
                            split_lo(plan[i + 1][0] if nxt else st, bb % 2, job, half, m + o, m + o, inc)
                    done[0] = upto + 1
                return splits

            def sum_squares(c0, src, n):
                return nc.vector.tensor_reduce(small[:, 0, c0:c0 + n], src, AX, ALU.add)

            def mixer(i):
                st, b, m = plan[i]
                z = kind_index(i)
                splits = splitter(i)

                def rope(t, o, src, ready):
                    c = cos_r[:, t:t + 1, :].broadcast_to([P, 2 * RH, RD // 2])
                    s_ = sin_r[:, t:t + 1, :].broadcast_to([P, 2 * RH, RD // 2])
                    xx = src.rearrange("p (g d) -> p g d", d=RD // 2)
                    r = rows[:, o, t, :]
                    link(nc.vector.tensor_tensor(r.rearrange("p (g d) -> p g d", d=RD // 2), xx, c, ALU.mult),
                         nc.vector.tensor_tensor(tmp[:, t, :].rearrange("p (g d) -> p g d", d=RD // 2), xx, s_, ALU.mult))
                    r = r.rearrange("p (h s d) -> p h s d", s=2, d=RD // 2)
                    w = tmp[:, t, :].rearrange("p (h s d) -> p h s d", s=2, d=RD // 2)
                    nc.vector.tensor_tensor(r[:, :, 0, :], r[:, :, 0, :], w[:, :, 1, :], ALU.subtract)
                    nc.vector.tensor_tensor(r[:, :, 1, :], r[:, :, 1, :], w[:, :, 0, :], ALU.add).then_inc(ready, 1)

                splits(5)
                dve.wait_ge(b4sq_ready, 2 * z + 2)
                link(sum_squares(0, sq[:, :, 0:S], 2),
                     sum_squares(2, sq[:, :, S:LAT], 2), sum_squares(4, sq[:, :, LAT:CB], 2))
                link(mean_eps(0, 2, S), mean_eps(2, 4, P), mean_eps(4, 6, ROPE))
                r = small[:, 3, :]
                rsqrt(6, r[:, 0:6])
                dve.wait_ge(mgain_loaded, 112 * (z + 1))
                dve.wait_ge(b4_ready, 2 * z + 2)
                for t in range(T):
                    for o, (c0, c1) in enumerate([(0, S), (S, LAT)]):
                        nc.vector.scalar_tensor_tensor(latn[:, t, c0:c1], b4[:, t, c0:c1],
                                                       r[:, 2 * o + t:2 * o + t + 1], g_lat[:, c0:c1],
                                                       ALU.mult, ALU.mult).then_inc(latn_ready, 1)
                link(*[nc.vector.scalar_tensor_tensor(krn[:, t, :], b4[:, t, LAT:CB], r[:, 4 + t:5 + t],
                                                      g_k[:, NOPE:QD], ALU.mult, ALU.mult) for t in range(T)])
                hr = ROPE // 2
                link(*[nc.vector.tensor_tensor(krt[:, :, k * hr:(k + 1) * hr], krn[:, :, k * hr:(k + 1) * hr], sin_m[:], ALU.mult)
                       for k in range(2)])
                link(*[nc.vector.tensor_tensor(krn[:, :, k * hr:(k + 1) * hr], krn[:, :, k * hr:(k + 1) * hr], cos_m[:], ALU.mult)
                       for k in range(2)])
                link(nc.vector.tensor_tensor(krn[:, :, 0:hr], krn[:, :, 0:hr], krt[:, :, hr:ROPE], ALU.subtract),
                     nc.vector.tensor_tensor(krn[:, :, hr:ROPE], krn[:, :, hr:ROPE], krt[:, :, 0:hr], ALU.add))
                splits(9)
                for t in range(T):
                    dve.wait_ge(lathi_ready, 2 * z + t + 1)
                    nc.vector.tensor_tensor(lat_lo[:, :, t * P:(t + 1) * P],
                                            bank[6 + t][:, 0:LAT].rearrange("p (k c) -> p k c", c=P),
                                            lat_hi[:, :, t * P:(t + 1) * P].bitcast(F32),
                                            ALU.subtract).then_inc(latlo_ready, 1)
                dve.wait_ge(split_used, OPEN + mid_pos(i, 3, 1) + 1)
                for t in range(T):
                    rope(t, 0, bank[2 + t][:], rowsq_ready)
                dve.wait_ge(rowsq_ready, 2 * z + 2)
                splits(13)
                dve.wait_ge(split_used, OPEN + mid_pos(i, 5, 1) + 1)
                for t in range(T):
                    rope(t, 1, bank[t][:], rowsk_ready)
                splits(17)
                dve.wait_ge(gth_ready, 2 * z + 2)
                link(*[nc.vector.scalar_tensor_tensor(gg[:, t, :], gg[:, t, :], 1.0, bank[t][:], ALU.add, ALU.mult)
                       for t in range(T)])
                for t in range(T):
                    nc.vector.scalar_tensor_tensor(gg[:, t, :], gg[:, t, :], 0.5, g_ret[:],
                                                   ALU.mult, ALU.mult).then_inc(gg_ready, 1)
                splits(21)
                for h in range(RH):
                    dve.wait_ge(rsc_ready, RH * z + h + 1)
                    nc.vector.tensor_tensor(scT[:, h, 0:S], bank[4 + h][:, 0:S], decay[:, h, :], ALU.mult)
                    nc.vector.tensor_tensor(scT[:, h, S:3 * P], bank[4 + h][:, S:3 * P], decay[:, h, 0:P],
                                            ALU.mult).then_inc(scT_ready, 1)
                splits(23)
                qv = q[:].rearrange("p t (h d) -> p (t h) d", d=QD)
                kv_ = kf[:].rearrange("p t (h d) -> p (t h) d", d=QD)
                kn = kvs[:].rearrange("p t (h d) -> p (t h) d", d=P)[:, :, 0:NOPE]
                sqv = sqq[:].rearrange("p t (h d) -> p (t h) d", d=QD)

                def spread(c0, n):
                    return r[:, c0:c0 + 16].rearrange("p (g o) -> p g o", o=1).broadcast_to([P, 16, n])

                def over_heads(g, n):
                    return g.rearrange("p (o d) -> p o d", o=1).broadcast_to([P, 16, n])

                dve.wait_ge(qsq_ready, 2 * z + 2)
                link(sum_squares(0, sqv[:, :, 0:NOPE], 16), sum_squares(16, sqv[:, :, NOPE:QD], 16))
                link(mean_eps(0, 16, NOPE), mean_eps(16, 32, ROPE))
                rsqrt(32, r[:, 0:32])
                link(nc.vector.tensor_tensor(qv[:, :, 0:NOPE], qv[:, :, 0:NOPE], spread(0, NOPE), ALU.mult),
                     nc.vector.tensor_tensor(qv[:, :, NOPE:QD], qv[:, :, NOPE:QD], spread(16, ROPE), ALU.mult))
                link(nc.vector.tensor_tensor(qv, qv, over_heads(g_q[:], QD), ALU.mult))
                for t in range(T):
                    qr_ = q[:, t, :].rearrange("p (h d) -> p h d", d=QD)[:, :, NOPE:QD]
                    w = qrt[:, t, :].rearrange("p (h d) -> p h d", d=ROPE)
                    c = cos_m[:, t:t + 1, :].broadcast_to([P, MH, hr])
                    s_ = sin_m[:, t:t + 1, :].broadcast_to([P, MH, hr])
                    link(*[nc.vector.tensor_tensor(w[:, :, k * hr:(k + 1) * hr], qr_[:, :, k * hr:(k + 1) * hr], s_, ALU.mult)
                           for k in range(2)])
                    link(*[nc.vector.tensor_tensor(qr_[:, :, k * hr:(k + 1) * hr], qr_[:, :, k * hr:(k + 1) * hr], c, ALU.mult)
                           for k in range(2)])
                    nc.vector.tensor_tensor(qr_[:, :, 0:hr], qr_[:, :, 0:hr], w[:, :, hr:ROPE], ALU.subtract)
                    nc.vector.tensor_tensor(qr_[:, :, hr:ROPE], qr_[:, :, hr:ROPE], w[:, :, 0:hr], ALU.add).then_inc(qf_ready, 1)
                for t in range(T):
                    dve.wait_ge(yrsq_ready, 2 * z + t + 1)
                    link(sum_squares(RH * t, sq[:, t, 0:512].rearrange("p (h d) -> p h d", d=RD), RH))
                link(mean_eps(0, T * RH, RD))
                rsqrt(T * RH, r[:, 0:T * RH])
                dve.wait_ge(gg_ready, 2 * z + 2)
                for t in range(T):
                    for h in range(RH):
                        c = slice(h * RD, (h + 1) * RD)
                        nc.vector.scalar_tensor_tensor(y[:, t, c], bank[4 + t][:, c], r[:, RH * t + h:RH * t + h + 1],
                                                       gg[:, t, c], ALU.mult, ALU.mult).then_inc(yret_ready, 1)
                dve.wait_ge(yret_ready, 8 * z + 8)
                dve.wait_ge(ksq_ready, 2 * z + 2)
                link(sum_squares(0, sqk[:].rearrange("p t (h d) -> p (t h) d", d=NOPE), 16))
                link(mean_eps(0, 16, NOPE))
                rsqrt(16, r[:, 0:16])
                link(nc.vector.tensor_tensor(kv_[:, :, 0:NOPE], kn, spread(0, NOPE), ALU.mult))
                link(nc.vector.tensor_tensor(kv_[:, :, 0:NOPE], kv_[:, :, 0:NOPE], over_heads(g_k[:, 0:NOPE], NOPE), ALU.mult))
                for t in range(T):
                    nc.vector.tensor_copy(kf[:, t, :].rearrange("p (h d) -> p h d", d=QD)[:, :, NOPE:QD],
                                          krn[:, t:t + 1, :].broadcast_to([P, MH, ROPE])).then_inc(kf_ready, 1)
                splits(29)
                for h in range(MH):
                    dve.wait_ge(msc_ready, MH * z + h + 1)
                    nc.vector.tensor_tensor(prob[:, h, :], bank[h][:, 0:3 * P], causal[:], ALU.add).then_inc(masked_ready, 1)
                dve.wait_ge(masked_ready, MH * (z + 1))
                mx = small[:, 5, 0:16].rearrange("p (h t) -> p h t", t=T)
                link(nc.vector.tensor_reduce(mx[:, :, 0], prob[:, :, 0:P], AX, ALU.max),
                     nc.vector.tensor_reduce(mx[:, :, 1], prob[:, :, P:3 * P], AX, ALU.max))
                nc.vector.tensor_scalar(small[:, 2, 0:16], small[:, 5, 0:16], -MLA_SCALE, None, ALU.mult).then_inc(negmax_ready, 1)
                for g in range(6):
                    dve.wait_ge(ptr_ready, 6 * z + g + 1)
                    nc.vector.tensor_copy(probT[:, 4 * g:4 * g + 4, :], bank[g % 4][:].rearrange("p (k c) -> p k c", c=P)).then_inc(pT_ready, 1)
                dve.wait_ge(exp_ready, 16 * z + 16)
                link(nc.vector.reciprocal(sums[:, 1, :, :], sums[:, 0, :, :]))
                dve.wait_ge(pv_ready, z + 1)
                for t in range(T):
                    nc.vector.tensor_tensor(y[:, t, 512:D].rearrange("p (h d) -> p h d", d=NOPE),
                                            bank[6 + t][:].rearrange("p (h d) -> p h d", d=NOPE),
                                            sums[:, 1, :, t:t + 1].broadcast_to([P, MH, NOPE]), ALU.mult).then_inc(ymla_ready, 1)
                columns(columns_index(i) + 1)
                splits(35)
                update_x(i, 1.0)

            def mixer2(i):
                st, b, m = plan[i]
                splits = splitter(i)
                r = small[:, 3, :]
                HUGE = 1e30

                def product(job):
                    dve.wait_ge(split_used, OPEN + mid_pos(i, job, 1) + 1)

                def chunks(w):
                    return w[:].rearrange("p h (n c) -> p (h n) c", c=GC)

                def column(w, c):
                    return chunks(w)[:, :, c:c + 1].broadcast_to([P, GH * NCH, GC])

                def forget(d):
                    dve.wait_ge(ne2_ready, 4 * d + 4)
                    e = g_ee[d]
                    link(nc.vector.tensor_scalar(g_t[:], e[:], HUGE, 1.0, ALU.min, ALU.add))
                    link(nc.vector.reciprocal(g_t[:], g_t[:]))
                    link(nc.vector.scalar_tensor_tensor(g_kk[:], e[:], HUGE, g_t[:], ALU.min, ALU.mult))
                    for h in range(GH):
                        nc.vector.tensor_scalar(g_kk[:, h, :], g_kk[:, h, :], lb[:, 1, d, h:h + 1], None, ALU.mult)
                    for h in range(GH):
                        ins = nc.vector.tensor_scalar(g_b[:, h, :], g_t[:, h, :], lb[:, 1, d, h:h + 1],
                                                      lb[:, 0, d, h:h + 1], ALU.mult, ALU.add)
                    ins.then_inc(f2_ready, 1)

                def log_sums(d):
                    dve.wait_ge(ln2_ready, d + 1)
                    flat = lambda w: w[:].rearrange("p h c -> p (h c)")
                    link(nc.vector.tensor_tensor_scan(flat(g_b), carry[:], flat(g_ee[d]), 0.0, ALU.mult, ALU.add))
                    if d:
                        link(nc.vector.tensor_tensor(chunks(g_t), column(g_b, GC - 1), chunks(g_b), ALU.subtract))
                        link(nc.vector.tensor_tensor(g_b[:], g_t[:], g_ee[d][:], ALU.add))
                    mid, last = (GC // 2, GC - 1) if d == 0 else (GC // 2 - 1, 0)
                    nc.vector.tensor_tensor(chunks(g_t), chunks(g_b), column(g_b, mid), ALU.subtract).then_inc(t2_ready, 1)
                    nc.vector.tensor_tensor(chunks(g_ee[d]), column(g_b, last), chunks(g_b), ALU.subtract).then_inc(t2_ready, 1)

                def weigh(d):
                    for n, (w, by) in enumerate([(g_qh, g_q2), (g_kh, g_kk), (g_qi[d], g_q2), (g_ks, g_kk)]):
                        dve.wait_ge(ex2_ready, 4 * d + n + 1)
                        nc.vector.tensor_tensor(w[:], w[:], by[:], ALU.mult).then_inc(dir_ready, 1)
                    dve.wait_ge(dir_ready, 4 * d + 4)
                    for n, (h0, h1) in enumerate(halves(d)):
                        to = chunks(g_kh1)[:, :, h0:h1]
                        (nc.vector.memset(to, 0.0) if n else nc.vector.tensor_copy(to, chunks(g_kh)[:, :, h0:h1])).then_inc(kh1_ready, 1)

                def mask_scores(d):
                    for t in range(T):
                        dve.wait_ge(asc2_ready, 2 * d + t + 1)
                        nc.vector.copy_predicated(g_aT[d][:, t, :].rearrange("p (h c) -> p h c", c=P),
                                                  reach[:, d:d + 1, :].broadcast_to([P, GH, P]),
                                                  bank[2 + t][:].rearrange("p (h c) -> p h c", c=P)).then_inc(aT2_ready, 1)

                def states(d):
                    dve.wait_ge(dec2_ready, d + 1)
                    for s_ in range(NCH - 1):
                        n = s_ if d == 0 else NCH - 1 - s_
                        k = 7 * d + s_
                        dve.wait_ge(kvp_ready, k + 1)
                        if k >= NST:
                            dve.wait_ge(inter_used, k - NST + 1)
                        if s_:
                            dve.wait_ge(state_ready, k)
                        src = bank[4 + k % 2]
                        for h in range(GH):
                            c = slice(h * GD, (h + 1) * GD)
                            if s_ == 0:
                                ins = nc.vector.tensor_copy(state[:, k % NST, c], src[:, c])
                            else:
                                ins = nc.vector.scalar_tensor_tensor(state[:, k % NST, c], state[:, (k - 1) % NST, c],
                                                                     dec[:, d, h, n:n + 1], src[:, c], ALU.mult, ALU.add)
                        ins.then_inc(state_ready, 1)

                dve.wait_ge(m2_loaded, 48)
                nc.vector.tensor_tensor(lb[:, 0, :, :], lb_in[:, :, 1, :], lb_in[:, :, 0, :], ALU.subtract).then_inc(lb_ready, 1)
                splits(5)
                dve.wait_ge(lbe_ready, 1)
                link(nc.vector.tensor_scalar(lb[:, 0, :, :], lb[:, 1, :, :], HUGE, 1.0, ALU.min, ALU.add))
                link(nc.vector.reciprocal(lb[:, 0, :, :], lb[:, 0, :, :]))
                link(nc.vector.scalar_tensor_tensor(lb[:, 1, :, :], lb[:, 1, :, :], HUGE, lb[:, 0, :, :], ALU.min, ALU.mult))
                forget(0)
                splits(9)
                dve.wait_ge(late_loaded, 32)
                log_sums(0)
                splits(13)
                dve.wait_ge(neq_ready, 4)
                link(nc.vector.tensor_scalar(g_q2[:], g_q2[:], HUGE, 1.0, ALU.min, ALU.add))
                link(nc.vector.reciprocal(g_q2[:], g_q2[:]))
                for h in range(GH):
                    nc.vector.scalar_tensor_tensor(g_q2[:, h, :], bank[h][:, 0:S], GD ** -0.5, g_q2[:, h, :],
                                                   ALU.mult, ALU.mult).then_inc(q2_ready, 1)
                dve.wait_ge(q2_ready, 4)
                weigh(0)
                splits(17)
                dve.wait_ge(dec2_ready, 1)
                forget(1)
                splits(25)
                log_sums(1)
                splits(29)
                dve.wait_ge(hgth_ready, 2)
                link(*[nc.vector.scalar_tensor_tensor(g_g[:, t, :], g_g[:, t, :], 1.0, bank[6 + t][:], ALU.add, ALU.mult)
                       for t in range(T)])
                for t in range(T):
                    nc.vector.scalar_tensor_tensor(g_g[:, t, :].rearrange("p (h d) -> p h d", d=GD),
                                                   g_g[:, t, :].rearrange("p (h d) -> p h d", d=GD), 0.5,
                                                   g_hn[:].rearrange("p (o d) -> p o d", o=1).broadcast_to([P, GH, GD]),
                                                   ALU.mult, ALU.mult).then_inc(gg2_ready, 1)
                dve.wait_ge(zero_ready, 2)
                mask_scores(0)
                weigh(1)
                splits(33)
                states(0)
                mask_scores(1)
                splits(37)
                states(1)
                nh = AH + AKV
                dve.wait_ge(asq_ready, 2)
                dve.wait_ge(late_loaded, 64)
                link(sum_squares(0, a_sq[:].rearrange("p t (h d) -> p (t h) d", d=AD), T * nh))
                link(mean_eps(0, T * nh, AD))
                rsqrt(T * nh, r[:, 0:T * nh])

                def heads(w, t):
                    return w[:, t, 0:640].rearrange("p (h d) -> p h d", d=AD)

                dve.wait_ge(aq2_ready, 4)
                link(*[nc.vector.tensor_tensor(heads(aqkv, t), heads(aqkv, t), r[:, nh * t:nh * (t + 1)].rearrange(
                    "p (h o) -> p h o", o=1).broadcast_to([P, nh, AD]), ALU.mult) for t in range(T)])
                link(*[nc.vector.tensor_tensor(heads(aqkv, t)[:, h0:h1, :], heads(aqkv, t)[:, h0:h1, :],
                                               g_64[:, e:e + 1, :].broadcast_to([P, h1 - h0, AD]), ALU.mult)
                       for t in range(T) for e, (h0, h1) in enumerate([(0, AH), (AH, nh)])])

                def pair(w, t, e):
                    return heads(w, t).rearrange("p h (d s) -> p h d s", s=2)[:, :, :, e]

                for o, dst in ((1, a_w), (0, aqkv)):
                    link(*[nc.vector.tensor_tensor(pair(dst, t, e), pair(aqkv, t, e),
                                                   axial[:, o, t:t + 1, :].broadcast_to([P, nh, AD // 2]), ALU.mult)
                           for t in range(T) for e in range(2)])
                for t in range(T):
                    nc.vector.tensor_tensor(pair(aqkv, t, 0), pair(aqkv, t, 0), pair(a_w, t, 1), ALU.subtract)
                    nc.vector.tensor_tensor(pair(aqkv, t, 1), pair(aqkv, t, 1), pair(a_w, t, 0), ALU.add).then_inc(aqk_ready, 1)
                splits(41)
                for t in range(T):
                    dve.wait_ge(osq_ready, t + 1)
                    link(sum_squares(GH * t, h_sq[:, t, :].rearrange("p (h d) -> p h d", d=GD), GH))
                link(mean_eps(0, T * GH, GD))
                rsqrt(T * GH, r[:, 0:T * GH])
                dve.wait_ge(gg2_ready, 2)
                for t in range(T):
                    for h in range(GH):
                        c = slice(h * GD, (h + 1) * GD)
                        nc.vector.scalar_tensor_tensor(yy[:, t, 512 + h * GD:512 + (h + 1) * GD], bank[t][:, c],
                                                       r[:, GH * t + h:GH * t + h + 1], g_g[:, t, c],
                                                       ALU.mult, ALU.mult).then_inc(yh_ready, 1)
                dve.wait_ge(yh_ready, 8)
                splits(45)
                for G in range(AKV):
                    c = slice(8 * G, 8 * G + 8)
                    tops = []
                    for h in range(4):
                        dve.wait_ge(as_ready, 4 * G + h + 1)
                        link(nc.vector.tensor_reduce(small[:, 5, 8 * G + 2 * h:8 * G + 2 * h + 2],
                                                     bank[2 + h][:].rearrange("p (t c) -> p t c", c=S), AX, ALU.max))
                    nc.vector.tensor_scalar(small[:, 2, c], small[:, 5, c], -(AD ** -0.5), None, ALU.mult).then_inc(amax_ready, 1)
                    if G:
                        dve.wait_ge(apv_ready, 1)
                    for h in range(4):
                        dve.wait_ge(aptr_ready, 4 * G + h + 1)
                        nc.vector.tensor_copy(a_pT[:, 4 * h:4 * h + 4, :],
                                              bank[2 + h][:].rearrange("p (k c) -> p k c", c=P)).then_inc(apT_ready, 1)
                dve.wait_ge(aexp_ready, 16)
                link(nc.vector.reciprocal(sums[:, 1, :, :], sums[:, 0, :, :]))
                dve.wait_ge(apv_ready, 2)
                for t in range(T):
                    nc.vector.tensor_tensor(yy[:, t, 0:512].rearrange("p (h d) -> p h d", d=AD),
                                            bank[t][:].rearrange("p (h d) -> p h d", d=AD),
                                            sums[:, 1, :, t:t + 1].broadcast_to([P, AH, AD]), ALU.mult).then_inc(ya_ready, 1)
                columns(columns_index(i) + 1)
                splits(49)
                for c in range(2):
                    product(22 + c)
                    link(*[nc.vector.scalar_tensor_tensor(merged[:, t, c * 512:(c + 1) * 512], gate[c][:, t, :], 1.0,
                                                          bank[2 * c + t][:], ALU.add, ALU.mult) for t in range(T)])
                splits(53)
                for c in range(2):
                    product(24 + c)
                    link(*[nc.vector.scalar_tensor_tensor(h_sq[:, t, :], gate[2 + c][:, t, :], 1.0,
                                                          bank[4 + 2 * c + t][:], ALU.add, ALU.mult) for t in range(T)])
                    for t in range(T):
                        w = merged[:, t, c * 512:(c + 1) * 512]
                        nc.vector.tensor_tensor(w, w, h_sq[:, t, :], ALU.add).then_inc(merged_ready, 1)
                    dve.wait_ge(merged_ready, 2 * c + 2)
                columns(columns_index(i) + 2)
                splits(59)
                update_x(i, 0.5)

            def norm_rows(i, permuted=False):
                dve.wait_ge(squares_ready, 2 * i + 2)
                link(mean_eps(0, T, D))
                r = small[:, 3, 0:T]
                rsqrt(T, r)
                dve.wait_ge(gain_loaded, 16 * (i + 1))
                for t in range(T):
                    to, xx, gg_ = xn[:, t, :], x[:, t, :], gain[:]
                    if permuted:
                        to = to.rearrange("p (k c) -> p c k", k=KC)
                        xx, gg_ = (w.rearrange("p (c k) -> p c k", k=KC) for w in (xx, gg_))
                    nc.vector.scalar_tensor_tensor(to, xx, r[:, t:t + 1], gg_, ALU.mult, ALU.mult).then_inc(xn_ready, 1)

            def experts(i):
                low = route[:, 0:NE]
                c = NE
                first_slot = route[:, c:c + MAXB + 1]
                c += MAXB + 1
                slot_of = route[:, c:c + MAXB + 1]
                c += MAXB + 1
                limits = route[:, c:c + S // BS - 1]
                c += S // BS - 1
                iota = route[:, c:c + NE]
                V = nc.vector

                def value(j, t=slice(0, T)):
                    return one[:, t, j:j + 1]

                def first_of(hit, tmp, width, o):
                    ids = low[:, 0:width].rearrange("p (o w) -> p o w", o=1).broadcast_to([P, T, width])
                    link(V.tensor_tensor(tmp, hit, ids, ALU.mult))
                    link(V.tensor_reduce(value(o), tmp, AX, ALU.min))
                    link(V.tensor_tensor(hit, ids, value(o).broadcast_to([P, T, width]), ALU.is_equal))

                dve.wait_ge(route_loaded, 96)
                dve.wait_ge(logits_done, 1)
                link(V.tensor_tensor(logits[:], bank[4][:, 0:T * LOGITS].rearrange("p (t n) -> p t n", t=T),
                                     b_router[:].rearrange("p (o n) -> p o n", o=1).broadcast_to([P, T, LOGITS]), ALU.add))
                gl = logits[:, :, 0:NG]
                link(V.tensor_reduce(value(0), gl, AX, ALU.max))
                V.tensor_tensor(g4[:, :, 0, :], gl, value(0).broadcast_to([P, T, NG]), ALU.subtract).then_inc(glogits_ready, 1)
                dve.wait_ge(gexp_ready, 1)
                ge, gh, gt = (g4[:, :, o, :] for o in (1, 2, 3))
                link(V.tensor_reduce(value(1), ge, AX, ALU.add), V.tensor_reduce(value(2), ge, AX, ALU.max))
                link(V.tensor_tensor(gh, ge, value(2).broadcast_to([P, T, NG]), ALU.is_equal),
                     V.reciprocal(value(1), value(1)))
                first_of(gh, gt, NG, 3)
                for t in range(T):
                    V.tensor_tensor(e8[:, t, :].rearrange("p (g e) -> p g e", g=NG),
                                    logits[:, t, NG:].rearrange("p (g e) -> p g e", g=NG),
                                    g4[:, t, 2, :].rearrange("p (g o) -> p g o", o=1).broadcast_to([P, NG, EG]),
                                    ALU.mult).then_inc(dve_step, 1)
                steps[0] += T
                dve.wait_ge(dve_step, steps[0])
                link(*[V.tensor_reduce(x8[:, t, 5, :], e8[:, t, :].rearrange("p (g e) -> p e g", g=NG), AX, ALU.add)
                       for t in range(T)])
                link(V.tensor_reduce(value(4), x8[:, :, 5, :], AX, ALU.max))
                V.tensor_tensor(x8[:, :, 0, :], x8[:, :, 5, :], value(4).broadcast_to([P, T, EG]),
                                ALU.subtract).then_inc(elogits_ready, 1)
                dve.wait_ge(eexp_ready, 1)
                ee, h1, h2, tm = (x8[:, :, o, :] for o in (1, 2, 3, 4))
                link(V.tensor_reduce(value(5), ee, AX, ALU.max))
                link(V.tensor_tensor(h1, ee, value(5).broadcast_to([P, T, EG]), ALU.is_equal))
                first_of(h1, tm, EG, 6)
                link(V.scalar_tensor_tensor(tm, h1, -4.0, ee, ALU.mult, ALU.add))
                link(V.tensor_reduce(value(7), tm, AX, ALU.max))
                link(V.tensor_tensor(h2, tm, value(7).broadcast_to([P, T, EG]), ALU.is_equal))
                first_of(h2, tm, EG, 8)
                link(V.tensor_tensor(value(9), value(5), value(7), ALU.add))
                link(V.reciprocal(value(9), value(9)))
                link(V.scalar_tensor_tensor(value(9), value(1), 0.5, value(9), ALU.mult, ALU.mult))
                link(V.tensor_tensor(value(10), value(5), value(9), ALU.mult), V.tensor_tensor(value(11), value(7), value(9), ALU.mult))
                link(*[V.tensor_tensor(pick[:, t, e, :].rearrange("p (g e) -> p g e", g=NG),
                                       g4[:, t, 2, :].rearrange("p (g o) -> p g o", o=1).broadcast_to([P, NG, EG]),
                                       x8[:, t, 2 + e, :].rearrange("p (o e) -> p o e", o=1).broadcast_to([P, NG, EG]), ALU.mult)
                       for t in range(T) for e in range(2)])
                V.tensor_tensor(both[:], pick[:, :, 0, :], pick[:, :, 1, :], ALU.add).then_inc(picks_ready, 1)
                dve.wait_ge(counts_done, 1)
                count = bank[5][:, 2 * NE:3 * NE]
                link(V.tensor_copy(blocks[:, 2, :], count))
                link(V.tensor_tensor(over[:], blocks[:, 2, :].rearrange("p (n o) -> p n o", o=1).broadcast_to([P, NE, S // BS - 1]),
                                     limits.rearrange("p (o n) -> p o n", o=1).broadcast_to([P, NE, S // BS - 1]), ALU.is_gt))
                link(V.tensor_reduce(blocks[:, 0, :], over[:], AX, ALU.add))
                link(V.tensor_scalar(blocks[:, 0, :], blocks[:, 0, :], 1.0, None, ALU.add), V.memset(blocks[:, 2, :], 1.0),
                     V.memset(cum[:, 0:1].bitcast(F32), 0.0))
                link(V.tensor_tensor_scan(blocks[:, 1, :], blocks[:, 2, :], blocks[:, 0, :], 0.0, ALU.mult, ALU.add))
                V.tensor_copy(cum[:, 1:NE + 1], blocks[:, 1, :]).then_inc(cum_ready, 1)
                link(V.tensor_tensor(blocks[:, 0, :], blocks[:, 1, :], blocks[:, 0, :], ALU.subtract))
                dve.wait_ge(cum_ready, 1)
                link(*[V.scalar_tensor_tensor(e8[:, t, :], blocks[:, 0, :], float(BS), bank[5][:, t * NE:(t + 1) * NE],
                                              ALU.mult, ALU.add) for t in range(T)])
                link(*[V.tensor_tensor(place[:, t, e, :], pick[:, t, e, :], e8[:, t, :], ALU.mult) for t in range(T) for e in range(2)])
                link(*[V.tensor_reduce(one[:, t, 2:4], place[:, t, :, :], AX, ALU.add) for t in range(T)])
                for v, col in enumerate((2, 3, 10, 11)):
                    for t in range(T):
                        ins = V.tensor_scalar(diag[:, 2 * v + t, :], ident[:], one[:, t, col:col + 1], None, ALU.mult)
                ins.then_inc(diag_ready, 1)
                link(*[V.tensor_tensor(rel[:, t, e, :], one[:, t, 2 + e:3 + e].broadcast_to([P, MAXB + 1]), first_slot, ALU.subtract)
                       for t in range(T) for e in range(2)])

                def tokens_to_slots(k, kk, value_):
                    for t in range(T):
                        V.tensor_scalar(take[:, t, :], iota, rel[:, t, 0, kk], None, ALU.is_equal)
                        ins = V.tensor_scalar(take2[:, t, :], iota, rel[:, t, 1, kk], None, ALU.is_equal)
                    ins.then_inc(take_step, 1)
                    dve.wait_ge(take_step, value_)
                    V.tensor_tensor(take[:], take[:], take2[:], ALU.add).then_inc(take_ready, 1)

                tokens_to_slots(0, slice(0, 1), 1)
                dve.wait_ge(acc_open, 1)
                dve.wait_ge(rows_ready, 2)
                total = dve.value_load(cum[0:1, NE:NE + 1], min_val=NE, max_val=MAXB)
                with dve.Fori(0, total) as k:
                    dve.wait_ge(gathered, k + 1)
                    tokens_to_slots(k + 1, bass.ds(k + 1, 1), k + 2)
                    dve.wait_ge(gu_done, k * 2 + 2)
                    V.tensor_copy(gu_sb[:, 1, :], GU[1][:]).then_inc(gu_copied, 1)
                    dve.wait_ge(given, k + 1)
                    V.scalar_tensor_tensor(give[:], rows4[:, 0, :], slot_of[:, bass.ds(k, 1)], rows4[:, 2, :], ALU.is_equal, ALU.mult)
                    V.scalar_tensor_tensor(give2[:], rows4[:, 1, :], slot_of[:, bass.ds(k, 1)], rows4[:, 3, :],
                                           ALU.is_equal, ALU.mult).then_inc(give_step, 1)
                    dve.wait_ge(give_step, k + 1)
                    V.tensor_tensor(give[:], give[:], give2[:], ALU.add).then_inc(give_ready, 1)
                    dve.wait_ge(eth_ready, k + 1)
                    V.scalar_tensor_tensor(e_sg[:].rearrange("p c s -> p (c s)"), e_th[:].rearrange("p c s -> p (c s)"), 1.0,
                                           bank[7][:, 0:FK * BS], ALU.add, ALU.mult).then_inc(esg_ready, 1)
                    dve.wait_ge(esg_ready, k + 1)
                    V.tensor_tensor(e_hid[:].rearrange("p c s -> p (c s)"), e_sg[:].rearrange("p c s -> p (c s)"),
                                    bank[7][:, FK * BS:2 * FK * BS], ALU.mult).then_inc(ehid_ready, 1)
                    dve.wait_ge(ydown_done, k * 2 + 2)
                    V.tensor_copy(y_sb[:, 512:D], GU[1][:]).then_inc(y_copied, 1)
                update_x(i, 1.0)

            def angles():
                dve.wait_ge(consts_loaded, 64)
                pf = small[:, 0, 0:T]
                link(nc.vector.tensor_copy(pf, pos_i[:]))
                link(*[nc.vector.tensor_scalar(ang[:, t, :], freq[:], pf[:, t:t + 1], None, ALU.mult) for t in range(T)])
                ROUND = 1.5 * 2.0 ** 23
                link(nc.vector.tensor_scalar(turns[:], ang[:], 1.0 / (2 * math.pi), ROUND, ALU.mult, ALU.add))
                link(nc.vector.tensor_scalar(turns[:], turns[:], -ROUND, None, ALU.add))
                for part in TWO_PI:
                    link(nc.vector.scalar_tensor_tensor(ang[:], turns[:], -part, ang[:], ALU.mult, ALU.add))
                nc.vector.tensor_scalar(ang[:], ang[:], PI_BELOW, -PI_BELOW, ALU.min, ALU.max).then_inc(angles_ready, 1)
                dve.wait_ge(sines_ready, 3)
                link(nc.vector.tensor_tensor(turns[:], turns[:], turns[:], ALU.mult))
                link(nc.vector.tensor_scalar(cos_r[:], turns[:, :, 0:RD // 2], -2.0, 1.0, ALU.mult, ALU.add),
                     nc.vector.tensor_scalar(cos_m[:], turns[:, :, RD // 2:NF], -2.0, 1.0, ALU.mult, ALU.add))

            for i, (st, b, m) in enumerate(plan):
                norm_rows(i)
                if i == 0:
                    first_splits(0)
                columns(columns_index(i))
                if i == 0:
                    angles()
                {"ffn": ffn, "mid": mixer, "mix2": mixer2}[st[0]](i)
            if moe:
                norm_rows(len(plan), permuted=True)
                nc.vector.memset(give[:], 0.0).then_inc(give_ready, 1)
                nc.vector.memset(y_sb[:], 0.0).then_inc(y_copied, 1)
                experts(len(plan))

        @block.tensor
        def _(pe):
            def three(o, sh, sl, mh, ml, first, last):
                nc.tensor.matmul(o, sh, mh, start=first, stop=False)
                nc.tensor.matmul(o, sh, ml, start=False, stop=False)
                return nc.tensor.matmul(o, sl, mh, start=False, stop=last)

            def columns(n, src, ready, values):
                for t in range(T):
                    pe.wait_ge(ready, values[t])
                    for h in range(2):
                        g = 2 * t + h
                        for k in range(4):
                            ins = nc.tensor.transpose(TR[g][:, k * P:(k + 1) * P],
                                                      src[:, t, (4 * h + k) * P:(4 * h + k + 1) * P], ident[:])
                        ins.then_inc(tr_ready, 1)
                pe.wait_ge(hlo_ready, 4 * n + 4)

            def ffn(i):
                st, b, m = plan[i]
                base = 22 * kind_index(i)

                def gate_up(o, mg, mu, sg_, su_, used=1):
                    for e, (mm, slot) in enumerate([(mg, sg_), (mu, su_)]):
                        pe.wait_ge(lo_ready, mm + 1)
                        wh = whi[:, slot % SLOTS, :].rearrange("p (k f) -> p k f", f=P)
                        wl = wlo[:, slot % SLOTS, :].rearrange("p (k f) -> p k f", f=P)
                        for k in range(KC):
                            ins = three(GU[o % 2][:, e * S:(e + 1) * S], wh[:, k, :], wl[:, k, :],
                                        hhi[:, k, :], hlo[:, k, :], k == 0, k == KC - 1)
                        ins.then_inc(split_used, used if e else 1)

                def down(c, o, mm, slot, first, last, used=1):
                    pe.wait_ge(lo_ready, mm + 1)
                    pe.wait_ge(actlo_ready, base + c + 1)
                    wh, wl = whi[:, slot % SLOTS, :], wlo[:, slot % SLOTS, :]
                    for t in range(T):
                        for h in range(2):
                            ins = three(Y[2 * t + h][:], act_hi[:, o % 2, t * P:(t + 1) * P],
                                        act_lo[:, o % 2, t * P:(t + 1) * P],
                                        wh[:, h * 512:(h + 1) * 512], wl[:, h * 512:(h + 1) * 512], first, last)
                    if last:
                        ins.then_inc(y_ready, 1)
                    else:
                        ins.then_inc(split_used, used)

                f4 = first4(m)
                gate_up(0, f4[0], f4[1], f4[0], f4[1], used=2)
                gate_up(1, f4[2], f4[3], f4[2], f4[3])

                def chunk(c, o, first=False):
                    down(c, o, m + 3 * c, m + 3 * o, first, False)
                    gate_up(o, m + 3 * c + 1, m + 3 * c + 2, m + 3 * o + 1, m + 3 * o + 2)

                chunk(0, 0, True)
                chunk(1, 1)
                with pe.Fori(0, 9) as r:
                    for o in range(2, 4):
                        chunk(r * 2 + o, o)
                down(20, 20, m + 60, m + 60, False, False)
                down(21, 21, m + 63, m + 63, False, True)

            def mixer(i):
                st, b, m = plan[i]
                z = kind_index(i)

                def use(ins, job, half):
                    last = (job, half) == (3 * batches(i) - 1, 1)
                    ins.then_inc(y_ready if last else split_used, 2 if (job, half) == (1, 0) else 1)

                def linear(jobs, banks, n):
                    halves = [(job, half) for job in jobs for half in range(2)]
                    if jobs[0] == 0:
                        halves = [(0, 0), (1, 0), (0, 1), (1, 1)]
                    for e, (job, half) in enumerate(halves):
                        mm = mid_pos(i, job, half)
                        pe.wait_ge(lo_ready, mm + 1)
                        wh = whi[:, mm % SLOTS, 0:2 * n].rearrange("p (k n) -> p k n", n=n)
                        wl = wlo[:, mm % SLOTS, 0:2 * n].rearrange("p (k n) -> p k n", n=n)
                        for kk in range(2):
                            k = 4 * (job - jobs[0]) + 2 * half + kk
                            for t in range(T):
                                c = slice(t * P, (t + 1) * P)
                                ins = three(banks[t][:, 0:n], hhi[:, k, c], hlo[:, k, c], wh[:, kk, :], wl[:, kk, :],
                                            e == 0 and kk == 0, e == 3 and kk == 1)
                        use(ins, job, half)

                linear((0, 1), bank[0:2], CB)
                linear((2, 3), bank[2:4], 512)
                pe.wait_ge(latn_ready, 4 * z + 4)
                for t in range(T):
                    for k in range(3):
                        ins = nc.tensor.transpose(bank[6 + t][:, k * P:(k + 1) * P], latn[:, t, k * P:(k + 1) * P], ident[:])
                    ins.then_inc(lattr_ready, 1)
                pe.wait_ge(b4sq_ready, 2 * z + 2)
                linear((4, 5), bank[0:2], 512)
                pe.wait_ge(rowsq_ready, 2 * z + 2)
                linear((6, 7), bank[2:4], 512)
                pe.wait_ge(rowsk_ready, 2 * z + 2)
                linear((8, 9), bank[0:2], 512)
                pe.wait_ge(latlo_ready, 2 * z + 2)
                for g in range(4):
                    o, t = g // 2, g % 2
                    for h in range(RH):
                        ins = nc.tensor.transpose(bank[4 + g][:, h * P:(h + 1) * P], rows[:, o, t, h * P:(h + 1) * P], ident[:])
                    ins.then_inc(rtr_ready, 1)
                pe.wait_ge(v_ready, 2 * z + 2)
                pe.wait_ge(gg_ready, 2 * z + 2)
                for k in range(2):
                    for half in range(2):
                        mm = mid_pos(i, 10 + k, half)
                        pe.wait_ge(lo_ready, mm + 1)
                        for t in range(T):
                            c = slice(t * P, (t + 1) * P)
                            ins = three(bank[2 * t + half][:, 0:LAT], lat_hi[:, k, c], lat_lo[:, k, c],
                                        whi[:, mm % SLOTS, 0:LAT], wlo[:, mm % SLOTS, 0:LAT], k == 0, k == 1)
                        use(ins, 10 + k, half)
                pe.wait_ge(qkT_ready, 4 * z + 4)
                for h in range(RH):
                    nc.tensor.matmul(bank[4 + h][:, 0:S], qkT[:, 1, h, 0:P], qkT[:, 0, h, :], start=True, stop=True)
                    nc.tensor.matmul(bank[4 + h][:, S:3 * P], qkT[:, 1, h, P:S], qkT[:, 0, h, P:S],
                                     start=True, stop=True).then_inc(rsc_ready, 1)
                pe.wait_ge(q_ready, 4 * z + 4)
                for job in (12, 13):
                    for half in range(2):
                        mm = mid_pos(i, job, half)
                        pe.wait_ge(lo_ready, mm + 1)
                        for t in range(T):
                            c = slice(t * P, (t + 1) * P)
                            ins = three(bank[2 * t + job - 12][:, half * S:(half + 1) * S], lat_hi[:, 2, c], lat_lo[:, 2, c],
                                        whi[:, mm % SLOTS, 0:S], wlo[:, mm % SLOTS, 0:S], True, True)
                        use(ins, job, half)
                pe.wait_ge(scT_ready, RH * (z + 1))
                for t in range(T):
                    for h in range(RH):
                        o = bank[4 + t][:, h * RD:(h + 1) * RD]
                        vh = slice(h * RD, (h + 1) * RD)
                        ins = nc.tensor.matmul(o, scT[:, h, t * P:(t + 1) * P], v[:, 0, vh], start=True, stop=t == 0)
                        if t:
                            ins = nc.tensor.matmul(o, scT[:, h, S:3 * P], v[:, 1, vh], start=False, stop=True)
                    ins.then_inc(yr_ready, 1)
                pe.wait_ge(yret_ready, 8 * z + 8)
                for g in range(8):
                    o, t, hh = g // 4, g // 2 % 2, g % 2
                    if g >= 4:
                        pe.wait_ge(mT_ready, 8 * z + g - 3)
                    pe.wait_ge(kf_ready if o else qf_ready, 2 * z + t + 1)
                    src = (q, kf)[o]
                    for h in range(4):
                        ins = nc.tensor.transpose(bank[4 + g % 4][0:QD, h * P:(h + 1) * P],
                                                  src[:, t, (4 * hh + h) * QD:(4 * hh + h + 1) * QD], ident[:])
                    ins.then_inc(mtr_ready, 1)
                pe.wait_ge(kv_ready, 4 * z + 4)
                pe.wait_ge(mT_ready, 8 * z + 8)
                for h in range(MH):
                    nc.tensor.matmul(bank[h][:, 0:P], qfT[0:QD, h, 0:P], kfT[0:QD, h, 0:P], start=True, stop=True)
                    nc.tensor.matmul(bank[h][:, P:3 * P], qfT[0:QD, h, P:S], kfT[0:QD, h, :],
                                     start=True, stop=True).then_inc(msc_ready, 1)
                for g in range(6):
                    pe.wait_ge(exp_ready, 16 * z + 2 * ((4 * g + 3) // 3 + 1))
                    if g >= 4:
                        pe.wait_ge(pT_ready, 6 * z + g - 3)
                    for o in range(4):
                        h, j = divmod(4 * g + o, 3)
                        ins = nc.tensor.transpose(bank[g % 4][:, o * P:(o + 1) * P], prob[:, h, j * P:(j + 1) * P], ident[:])
                    ins.then_inc(ptr_ready, 1)
                pe.wait_ge(pT_ready, 6 * z + 6)
                for t in range(T):
                    for h in range(MH):
                        o = bank[6 + t][:, h * NOPE:(h + 1) * NOPE]
                        c = slice(h * P + NOPE, (h + 1) * P)
                        ins = nc.tensor.matmul(o, probT[:, 3 * h + t, :], kvs[:, 0, c], start=True, stop=t == 0)
                        if t:
                            ins = nc.tensor.matmul(o, probT[:, 3 * h + 2, :], kvs[:, 1, c], start=False, stop=True)
                ins.then_inc(pv_ready, 1)
                columns(columns_index(i) + 1, y, ymla_ready, [2 * z + 2] * T)
                for c in range(2):
                    linear((14 + 2 * c, 15 + 2 * c), (Y[c], Y[2 + c]), 512)

            def mixer2(i):
                st, b, m = plan[i]

                def use(ins, job, half):
                    last = (job, half) == (3 * batches(i) - 1, 1)
                    ins.then_inc(y_ready if last else split_used, 2 if (job, half) == (1, 0) else 1)

                def halves_of(jobs):
                    return [(0, 0), (1, 0), (0, 1), (1, 1)] if jobs[0] == 0 else [(j, h) for j in jobs for h in range(2)]

                def split_parts(job, half, n):
                    mm = mid_pos(i, job, half)
                    pe.wait_ge(lo_ready, mm + 1)
                    return [w[:, mm % SLOTS, 0:2 * n].rearrange("p (k n) -> p k n", n=n) for w in (whi, wlo)]

                def linear(jobs, banks, n, k0=0):
                    every = halves_of(jobs)
                    for e, (job, half) in enumerate(every):
                        wh, wl = split_parts(job, half, n)
                        for kk in range(2):
                            k = k0 + 4 * (job - jobs[0]) + 2 * half + kk
                            for t in range(T):
                                c = slice(t * P, (t + 1) * P)
                                ins = three(banks[t][:, 0:n], hhi[:, k, c], hlo[:, k, c], wh[:, kk, :], wl[:, kk, :],
                                            e == 0 and kk == 0, e == len(every) - 1 and kk == 1)
                        use(ins, job, half)

                def linear_columns(jobs, banks):
                    for e, (job, half) in enumerate(halves_of(jobs)):
                        wh, wl = split_parts(job, half, 512)
                        for kk in range(2):
                            k = 4 * (job - jobs[0]) + 2 * half + kk
                            for h in range(GH):
                                c = slice(h * GD, (h + 1) * GD)
                                ins = three(banks[h][:, 0:S], wh[:, kk, c], wl[:, kk, c], hhi[:, k, :], hlo[:, k, :],
                                            e == 0 and kk == 0, e == 3 and kk == 1)
                        use(ins, job, half)

                def state_rows(d):
                    pe.wait_ge(dir_ready, 4 * d + 4)
                    pe.wait_ge(aT2_ready, 2 * d)  if d else None
                    for t in range(T):
                        for h in range(GH):
                            ins = nc.tensor.transpose(bank[2 + t][:, h * P:(h + 1) * P], g_ks[:, h, t * P:(t + 1) * P], ident[:])
                        ins.then_inc(kst_ready, 1)

                def scores(d):
                    pe.wait_ge(ksr_ready, 2 * d + 2)
                    pe.wait_ge(kh1_ready, 2 * d + 2)
                    for t in range(T):
                        c = slice(t * P, (t + 1) * P)
                        for h in range(GH):
                            for kh, (h0, h1) in zip((g_kh1, g_kh), halves(d)):
                                o, w = (v_.rearrange("p (n c) -> p n c", c=GC)[:, :, h0:h1]
                                        for v_ in (bank[2 + t][:, h * P:(h + 1) * P], g_qh[:, h, c]))
                                ins = nc.tensor.matmul(o, kh[:, h, c], w, start=True, stop=True)
                        ins.then_inc(asc2_ready, 1)

                def within(d):
                    for t in range(T):
                        pe.wait_ge(aT2_ready, 2 * d + t + 1)
                        for h in range(GH):
                            c = slice(h * P, (h + 1) * P)
                            nc.tensor.matmul(bank[t][:, c], g_aT[d][:, t, c], g_v[:, t, c],
                                             start=d == 0 and h == 0, stop=False, skip_group_check=True)

                def across(d):
                    for s_ in range(NCH):
                        n = s_ if d == 0 else NCH - 1 - s_
                        t, j = divmod(n, CPT)
                        k = 7 * d + s_
                        pj = slice(GC * j, GC * (j + 1))
                        if s_ < NCH - 1:
                            if k >= 2:
                                pe.wait_ge(state_ready, k - 1)
                            for h in range(GH):
                                c = slice(h * GD, (h + 1) * GD)
                                ins = nc.tensor.matmul(bank[4 + k % 2][:, c], g_ksr[d][pj, t, c], g_v[pj, t, c], start=True, stop=True)
                            ins.then_inc(kvp_ready, 1)
                        if s_:
                            pe.wait_ge(state_ready, k)
                            for h in range(GH):
                                c = slice(h * GD, (h + 1) * GD)
                                ins = nc.tensor.matmul(bank[t][pj, c], g_qi[d][:, h, n * GC:(n + 1) * GC],
                                                       state[:, (k - 1) % NST, c], start=False, stop=False, skip_group_check=True)
                            ins.then_inc(o2_ready if d and s_ == NCH - 1 else inter_used, 1)

                def gates(c):
                    pe.wait_ge(gate_th_ready, 2 * c) if c else pe.wait_ge(gg2_ready, 2)
                    linear((14 + 2 * c, 15 + 2 * c), bank[6:8], 512)

                linear_columns((0, 1), bank[0:4])
                linear_columns((2, 3), bank[4:8])
                pe.wait_ge(ne2_ready, 4)
                linear_columns((4, 5), bank[0:4])
                pe.wait_ge(ne2_ready, 8)
                linear((6, 7), bank[4:6], 512)
                linear((8, 9), bank[6:8], 512)
                pe.wait_ge(v2_ready, 2)
                linear((10, 11), bank[4:6], 256)
                pe.wait_ge(aq2_ready, 2)
                linear((12, 13), bank[6:8], 512)
                pe.wait_ge(q2_ready, 4)
                state_rows(0)
                scores(0)
                gates(0)
                within(0)
                pe.wait_ge(aq2_ready, 4)
                across(0)
                state_rows(1)
                scores(1)
                gates(1)
                within(1)
                across(1)
                gates(2)
                for g in range(6):
                    t, e = divmod(g, 3)
                    pe.wait_ge(aqk_ready, 2)
                    if g >= 4:
                        pe.wait_ge(aT_ready, g - 3)
                    for h in range(4 if e < 2 else 2):
                        ins = nc.tensor.transpose(bank[2 + g % 4][0:AD, h * P:(h + 1) * P],
                                                  aqkv[:, t, (4 * e + h) * AD:(4 * e + h + 1) * AD], ident[:])
                    ins.then_inc(atr_ready, 1)
                gates(3)
                for G in range(AKV):
                    pe.wait_ge(aT_ready, 6)
                    if G:
                        pe.wait_ge(apT_ready, 4)
                    for h in range(4):
                        for t in range(T):
                            ins = nc.tensor.matmul(bank[2 + h][:, t * S:(t + 1) * S], aT_q[0:AD, 4 * G + h, t * P:(t + 1) * P],
                                                   aT_k[0:AD, G, :], start=True, stop=True)
                        ins.then_inc(as_ready, 1)
                    for h in range(4):
                        pe.wait_ge(aexp_ready, 8 * G + 2 * h + 2)
                        for k in range(4):
                            ins = nc.tensor.transpose(bank[2 + h][:, k * P:(k + 1) * P],
                                                      a_pr[:, h, k // 2, (k % 2) * P:(k % 2 + 1) * P], ident[:])
                        ins.then_inc(aptr_ready, 1)
                    pe.wait_ge(apT_ready, 4 * G + 4)
                    pe.wait_ge(yh_ready, 8)
                    for t in range(T):
                        for h in range(4):
                            for k in range(2):
                                ins = nc.tensor.matmul(bank[t][:, (4 * G + h) * AD:(4 * G + h + 1) * AD], a_pT[:, 4 * h + 2 * t + k, :],
                                                       aqkv[:, k, 640 + G * AD:640 + (G + 1) * AD], start=k == 0, stop=k == 1)
                    ins.then_inc(apv_ready, 1)
                pe.wait_ge(gate_th_ready, 8)
                columns(columns_index(i) + 1, yy, ya_ready, [2, 2])
                for c in range(2):
                    linear((22 + c,), bank[2 * c:2 * c + 2], 512)
                for c in range(2):
                    linear((24 + c,), bank[4 + 2 * c:6 + 2 * c], 512, k0=4)
                columns(columns_index(i) + 2, merged, merged_ready, [4, 4])
                for c in range(2):
                    linear((26 + 2 * c, 27 + 2 * c), (Y[c], Y[2 + c]), 512)

            def experts(i):
                for t in range(T):
                    pe.wait_ge(xn_ready, 2 * i + t + 1)
                    for h in range(2):
                        for k in range(4):
                            ins = nc.tensor.transpose(TR[2 * t + h][:, k * P:(k + 1) * P],
                                                      xn[:, t, (4 * h + k) * P:(4 * h + k + 1) * P], ident[:])
                        ins.then_inc(tr_ready, 1)
                pe.wait_ge(hhi_ready, 4 * columns_index(i) + 4)
                pe.wait_ge(route_loaded, 96)
                for t in range(T):
                    for w, c0, c1 in ((w_group, 0, NG), (w_router, NG, LOGITS)):
                        for k in range(KC):
                            ins = nc.tensor.matmul(bank[4][:, t * LOGITS + c0:t * LOGITS + c1], hcol[:, k, t * P:(t + 1) * P],
                                                   w[:, k, :], start=k == 0, stop=k == KC - 1)
                ins.then_inc(logits_done, 1)
                pe.wait_ge(give_ready, 1)
                pe.wait_ge(y_copied, 1)

                def scatter(first, last):
                    for t in range(T):
                        for h in range(2):
                            ins = nc.tensor.matmul(Y[2 * t + h][:], give[:, t * P:(t + 1) * P], y_sb[:, h * 512:(h + 1) * 512],
                                                   start=first, stop=last, skip_group_check=True)
                    return ins

                scatter(True, False).then_inc(acc_open, 1)
                before, ones, stack = square[:, 0:P], square[:, P:2 * P], square[:, 2 * P:]
                pe.wait_ge(picks_ready, 1)
                nc.tensor.matmul(bank[5][:, 0:NE], before, both[:, 0, :], start=True, stop=True)
                nc.tensor.matmul(bank[5][:, NE:2 * NE], ones, both[:, 0, :], start=True, stop=False)
                nc.tensor.matmul(bank[5][:, NE:2 * NE], before, both[:, 1, :], start=False, stop=True)
                nc.tensor.matmul(bank[5][:, 2 * NE:3 * NE], ones, both[:, 0, :], start=True, stop=False)
                nc.tensor.matmul(bank[5][:, 2 * NE:3 * NE], ones, both[:, 1, :], start=False, stop=True).then_inc(counts_done, 1)
                pe.wait_ge(diag_ready, 1)
                for h in range(2):
                    ins = nc.tensor.matmul(bank[6 + h][:], ones, diag[:, 4 * h:4 * h + 4, :].rearrange("p v c -> p (v c)"),
                                           start=True, stop=True)
                ins.then_inc(rows_done, 1)

                def gather():
                    for k in range(KC):
                        for t in range(T):
                            ins = nc.tensor.matmul(bank[6][:, k * BS:(k + 1) * BS], xn[:, t, k * P:(k + 1) * P], take[:, t, :],
                                                   start=t == 0, stop=t == 1)
                    ins.then_inc(gathered, 1)

                pe.wait_ge(take_ready, 1)
                pe.wait_ge(rows_ready, 2)
                gather()

                def block_of(k, j, landed):
                    wg, wu, wd = (expert_w[j][w][:].rearrange("p (k n) -> p k n", k=n) for w, n in enumerate((KC, KC, FK)))
                    pe.wait_ge(gu_landed[j], landed * 2)
                    pe.wait_ge(he_ready, k + 1)
                    pe.wait_ge(y_copied, k * 2 + 1)
                    for o, w in enumerate((wg, wu)):
                        for c in range(KC):
                            q_ = c % Q
                            ins = nc.tensor.matmul(GU[o][BS * q_:BS * (q_ + 1), :], h_e[:, c, :], w[:, c, :], start=c < Q, stop=c >= Q,
                                                   tile_position=(0, BS * q_))
                        ins.then_inc(gu_done, 1)
                    pe.wait_ge(give_ready, k + 1)
                    scatter(False, False).then_inc(given, 1)
                    pe.wait_ge(gu_copied, k * 2 + 2)
                    for o in range(2):
                        for c in range(FK):
                            lhs = gu_sb[:, o, :].rearrange("p (m c) -> p c m", c=FK)[:, c, :]
                            ins = nc.tensor.matmul(bank[7][:, (FK * o + c) * BS:(FK * o + c + 1) * BS], lhs, stack, start=True, stop=True)
                    ins.then_inc(turned, 1)
                    pe.wait_ge(take_ready, k + 2)
                    gather()
                    pe.wait_ge(down_landed[j], landed)
                    pe.wait_ge(ehid_ready, k + 1)
                    for h in range(2):
                        for c in range(FK):
                            ins = nc.tensor.matmul(GU[h][BS * c:BS * (c + 1), :], e_hid[:, c, :], wd[:, c, h * 512:(h + 1) * 512],
                                                   start=True, stop=True, tile_position=(0, BS * c))
                        ins.then_inc(ydown_done, 1)

                def expert(e, j, round_):
                    lo = pe.value_load(cum[0:1, bass.ds(e, 1)], min_val=0, max_val=MAXB)
                    hi = pe.value_load(cum[0:1, bass.ds(e + 1, 1)], min_val=1, max_val=MAXB)
                    with pe.Fori(lo, hi) as k:
                        block_of(k, j, (round_ + 1) * 16)

                pe.wait_ge(cum_ready, 1)
                with pe.Fori(0, NE // RING) as r:
                    for j in range(RING):
                        expert(r * RING + j, j, r)
                for e in range(NE // RING * RING, NE):
                    expert(e, e % RING, e // RING)
                total = pe.value_load(cum[0:1, NE:NE + 1], min_val=NE, max_val=MAXB)
                pe.wait_ge(give_ready, total + 1)
                pe.wait_ge(y_copied, total * 2 + 1)
                scatter(False, True).then_inc(y_ready, 1)

            pe.wait_ge(x_loaded, 32)
            nc.tensor.transpose(bank[0][:, 0:P], ident[:], ident[:]).then_inc(split_used, OPEN)
            for i, (st, b, m) in enumerate(plan):
                columns(columns_index(i), xn, xn_ready, [2 * i + t + 1 for t in range(T)])
                {"ffn": ffn, "mid": mixer, "mix2": mixer2}[st[0]](i)
            if moe:
                experts(len(plan))


STAGES = [st for l in range(DEPTH) for st in (("ffn", l, 1), ("mid", l), ("ffn", l, 2))] + [("mix2",), ("moe",)]


def kernel(**inputs):
    import concourse.bacc as bacc
    from concourse.bass_utils import run_bass_kernel_spmd

    arrays = {k: np.ascontiguousarray(v) for k, v in inputs.items() if not k.startswith("lb_")}
    arrays["positions"] = np.ascontiguousarray(np.asarray(inputs["positions"])[0].reshape(T, P).T)
    bounds = np.stack([np.asarray(inputs["lb_fwd_2"]), np.asarray(inputs["lb_bwd_2"])])
    arrays["lb_cols"] = np.ascontiguousarray(bounds.reshape(2, 2, GH, GD).transpose(3, 0, 1, 2))
    arrays.update(constants())

    nc = bacc.Bacc("TRN2", target_bir_lowering=False, num_devices=1)
    aps = {k: nc.dram_tensor(f"in_{k}", v.shape, mybir.dt.from_np(v.dtype), kind="ExternalInput").ap() for k, v in arrays.items()}
    out = nc.dram_tensor("out", (1, S, D), F32, kind="ExternalOutput").ap()
    program(nc, aps, out, STAGES)
    r = run_bass_kernel_spmd(nc, [{f"in_{k}": v for k, v in arrays.items()}], core_ids=[0])
    return r.results[0]["out"]
```
